# Optimizing a Trainium2 kernel written in Bass

```python
import math
import jax, jax.numpy as jnp
from jax import lax
import numpy as np

D_MODEL = 2048
BATCH = 1
SEQ = 256
DEPTH = 2

N_MIXERS = 2
N_HEADS = 16
HEAD_DIM = D_MODEL // N_HEADS
DSA_KV_HEADS = 4
DSA_GROUP = N_HEADS // DSA_KV_HEADS
IDX_HEADS = 16
IDX_DIM = 128
TOPK_MAX = 256
Q_BLOCK = 128
D_FF = 5632
CONV_WIDTH = 3
ROPE_THETA = 10000.0
NORM_EPS = 1e-6
N_A_LAYERS = (DEPTH + 1) // 2
N_B_LAYERS = DEPTH // 2

DSA_Q_COLS = N_HEADS * HEAD_DIM
DSA_KV_COLS = DSA_KV_HEADS * HEAD_DIM
DSA_QI_COLS = IDX_HEADS * IDX_DIM
DSA_KI_COLS = IDX_DIM
DSA_WI_COLS = IDX_HEADS
DSA_IN_COLS = DSA_Q_COLS + 2 * DSA_KV_COLS + DSA_QI_COLS + DSA_KI_COLS + DSA_WI_COLS

kernel_name = "hybrid_stickbreaking_dsa_convffn"

def _rmsnorm(x, g):
    xf = x.astype(jnp.float32)
    y = xf * lax.rsqrt(jnp.mean(xf * xf, axis=-1, keepdims=True) + NORM_EPS)
    return (y * g.astype(jnp.float32)).astype(x.dtype)

def _rope_tables(seq_len, dim):
    inv_freq = 1.0 / (ROPE_THETA ** (jnp.arange(0, dim, 2, dtype=jnp.float32) / dim))
    ang = jnp.arange(seq_len, dtype=jnp.float32)[:, None] * inv_freq[None, :]
    return jnp.cos(ang), jnp.sin(ang)

def _rope(x, cos, sin):
    half = x.shape[-1] // 2
    shp = (x.shape[1],) + (1,) * (x.ndim - 3) + (half,)
    c = cos.reshape(shp).astype(x.dtype)
    s = sin.reshape(shp).astype(x.dtype)
    x1, x2 = x[..., :half], x[..., half:]
    return jnp.concatenate([x1 * c - x2 * s, x2 * c + x1 * s], axis=-1)

def _stick_breaking_attention(h, w_qkv, w_o):
    B, S, _ = h.shape
    qkv = (h @ w_qkv).reshape(B, S, 3, N_HEADS, HEAD_DIM)
    q = qkv[:, :, 0].transpose(0, 2, 1, 3)
    k = qkv[:, :, 1].transpose(0, 2, 1, 3)
    v = qkv[:, :, 2].transpose(0, 2, 1, 3)
    nb = S // Q_BLOCK
    q_blocks = q.reshape(B, N_HEADS, nb, Q_BLOCK, HEAD_DIM).transpose(2, 0, 1, 3, 4)
    s_pos = jnp.arange(S)
    scale = 1.0 / math.sqrt(HEAD_DIM)

    def one_block(args):
        qb, bi = args
        t_pos = bi * Q_BLOCK + jnp.arange(Q_BLOCK)
        z = jnp.einsum('bhtd,bhsd->bhts', qb, k).astype(jnp.float32) * scale
        mask = (s_pos[None, :] < t_pos[:, None])[None, None]
        neg_log_1m_beta = jnp.where(mask, jax.nn.softplus(z), 0.0)
        between = lax.cumsum(neg_log_1m_beta, axis=3, reverse=True) - neg_log_1m_beta
        log_a = jax.nn.log_sigmoid(z) - between
        a = jnp.where(mask, jnp.exp(log_a), 0.0)
        return jnp.einsum('bhts,bhsd->bhtd', a.astype(v.dtype), v)

    out = lax.map(one_block, (q_blocks, jnp.arange(nb)))
    out = out.transpose(1, 0, 3, 2, 4).reshape(B, S, N_HEADS * HEAD_DIM)
    return out @ w_o

def _dsa_attention(h, w_in, q_norm_g, k_norm_g, ik_norm_g, w_o):
    B, S, _ = h.shape
    proj = h @ w_in
    o0 = DSA_Q_COLS
    o1 = o0 + DSA_KV_COLS
    o2 = o1 + DSA_KV_COLS
    o3 = o2 + DSA_QI_COLS
    o4 = o3 + DSA_KI_COLS
    q = proj[..., :o0].reshape(B, S, N_HEADS, HEAD_DIM)
    k = proj[..., o0:o1].reshape(B, S, DSA_KV_HEADS, HEAD_DIM)
    v = proj[..., o1:o2].reshape(B, S, DSA_KV_HEADS, HEAD_DIM)
    qi = proj[..., o2:o3].reshape(B, S, IDX_HEADS, IDX_DIM)
    ki = proj[..., o3:o4]
    wi = proj[..., o4:]

    cos, sin = _rope_tables(S, HEAD_DIM)
    q = _rope(_rmsnorm(q, q_norm_g), cos, sin)
    k = _rope(_rmsnorm(k, k_norm_g), cos, sin)
    cos_i, sin_i = _rope_tables(S, IDX_DIM)
    qi = _rope(qi, cos_i, sin_i)
    ki = _rope(_rmsnorm(ki, ik_norm_g), cos_i, sin_i)

    topk = min(TOPK_MAX, S // 4)
    nb = S // Q_BLOCK
    q_b = q.reshape(B, nb, Q_BLOCK, N_HEADS, HEAD_DIM).swapaxes(0, 1)
    qi_b = qi.reshape(B, nb, Q_BLOCK, IDX_HEADS, IDX_DIM).swapaxes(0, 1)
    wi_b = wi.reshape(B, nb, Q_BLOCK, IDX_HEADS).swapaxes(0, 1)
    s_pos = jnp.arange(S)
    b_idx = jnp.arange(B)[:, None, None]
    idx_scale = 1.0 / math.sqrt(IDX_DIM)
    head_w_scale = 1.0 / math.sqrt(IDX_HEADS)
    attn_scale = 1.0 / math.sqrt(HEAD_DIM)

    def one_block(args):
        qb, qib, wib, bi = args
        t_pos = bi * Q_BLOCK + jnp.arange(Q_BLOCK)
        logits = jnp.einsum('bthe,bse->bths', qib, ki).astype(jnp.float32) * idx_scale
        score = jnp.einsum('bths,bth->bts', jax.nn.relu(logits),
                           wib.astype(jnp.float32)) * head_w_scale
        admissible = (s_pos[None, :] <= t_pos[:, None])[None]
        score = jnp.where(admissible, score, -jnp.inf)
        _, sel = lax.top_k(score, topk)
        k_sel = k[b_idx, sel]
        v_sel = v[b_idx, sel]
        valid = sel <= t_pos[None, :, None]
        qg = qb.reshape(B, Q_BLOCK, DSA_KV_HEADS, DSA_GROUP, HEAD_DIM)
        s = jnp.einsum('btgrd,btkgd->btgrk', qg, k_sel).astype(jnp.float32) * attn_scale
        s = jnp.where(valid[:, :, None, None, :], s, -jnp.inf)
        p = jax.nn.softmax(s, axis=-1)
        o = jnp.einsum('btgrk,btkgd->btgrd', p.astype(v.dtype), v_sel)
        return o.reshape(B, Q_BLOCK, N_HEADS * HEAD_DIM)

    out = lax.map(one_block, (q_b, qi_b, wi_b, jnp.arange(nb)))
    out = out.swapaxes(0, 1).reshape(B, S, N_HEADS * HEAD_DIM)
    return out @ w_o

def _conv_ffn(h, w_up, conv_w, conv_b, w_down):
    u = h @ w_up
    S = u.shape[1]
    up = jnp.pad(u, ((0, 0), (CONV_WIDTH - 1, 0), (0, 0)))
    c = conv_b
    for j in range(CONV_WIDTH):
        c = c + up[:, j:j + S] * conv_w[j]
    gate, val = jnp.split(c, 2, axis=-1)
    return (jax.nn.silu(gate) * val) @ w_down

def setup_inputs(seed: int = 0) -> dict:
    key = jax.random.key(seed)
    ks = jax.random.split(key, 16)
    f32 = jnp.float32

    def nrm(k, shape, fan_in):
        return jax.random.normal(k, shape, f32) * (fan_in ** -0.5)

    def gain(k, shape):
        return 1.0 + 0.02 * jax.random.normal(k, shape, f32)

    return {
        "x": jax.random.normal(ks[0], (BATCH, SEQ, D_MODEL), f32),
        "attn_norm_g": gain(ks[1], (DEPTH, D_MODEL)),
        "ffn_norm_g": gain(ks[2], (DEPTH, D_MODEL)),
        "sb_w_qkv": nrm(ks[3], (N_A_LAYERS, D_MODEL, 3 * N_HEADS * HEAD_DIM), D_MODEL),
        "sb_w_o": nrm(ks[4], (N_A_LAYERS, N_HEADS * HEAD_DIM, D_MODEL), N_HEADS * HEAD_DIM),
        "dsa_w_in": nrm(ks[5], (N_B_LAYERS, D_MODEL, DSA_IN_COLS), D_MODEL),
        "dsa_q_norm_g": gain(ks[6], (N_B_LAYERS, HEAD_DIM)),
        "dsa_k_norm_g": gain(ks[7], (N_B_LAYERS, HEAD_DIM)),
        "dsa_ik_norm_g": gain(ks[8], (N_B_LAYERS, IDX_DIM)),
        "dsa_w_o": nrm(ks[9], (N_B_LAYERS, N_HEADS * HEAD_DIM, D_MODEL), N_HEADS * HEAD_DIM),
        "ffn_w_up": nrm(ks[10], (DEPTH, D_MODEL, 2 * D_FF), D_MODEL),
        "ffn_conv_w": nrm(ks[11], (DEPTH, CONV_WIDTH, 2 * D_FF), CONV_WIDTH),
        "ffn_conv_b": 0.01 * jax.random.normal(ks[12], (DEPTH, 2 * D_FF), f32),
        "ffn_w_down": nrm(ks[13], (DEPTH, D_FF, D_MODEL), D_FF),
    }

def reference(x, attn_norm_g, ffn_norm_g, sb_w_qkv, sb_w_o, dsa_w_in, dsa_q_norm_g,
              dsa_k_norm_g, dsa_ik_norm_g, dsa_w_o, ffn_w_up, ffn_conv_w, ffn_conv_b,
              ffn_w_down):
    for i in range(DEPTH):
        h = _rmsnorm(x, attn_norm_g[i])
        j = i // N_MIXERS
        if i % N_MIXERS == 0:
            mix = _stick_breaking_attention(h, sb_w_qkv[j], sb_w_o[j])
        else:
            mix = _dsa_attention(h, dsa_w_in[j], dsa_q_norm_g[j], dsa_k_norm_g[j],
                                 dsa_ik_norm_g[j], dsa_w_o[j])
        x = x + mix
        h = _rmsnorm(x, ffn_norm_g[i])
        x = x + _conv_ffn(h, ffn_w_up[i], ffn_conv_w[i], ffn_conv_b[i], ffn_w_down[i])
    return x


_drawn_inputs = setup_inputs


def setup_inputs(seed=0):
    import zlib

    import numpy as np

    out = dict(_drawn_inputs(seed))
    spreads = {}
    factors = {'dsa_q_norm_g': 8.0, 'dsa_k_norm_g': 8.0, 'dsa_ik_norm_g': 3.512, 'ffn_conv_b': 3.808}
    for name, (base, spread) in spreads.items():
        noise = np.random.default_rng([zlib.crc32(name.encode()), seed]).standard_normal(out[name].shape)
        drawn = base * np.exp(spread * noise) if base else spread * noise
        out[name] = __import__('jax').numpy.asarray(drawn.astype(out[name].dtype))
    for name, factor in factors.items():
        out[name] = (out[name] * factor).astype(out[name].dtype)
    return out
```

```python
from contextlib import ExitStack

import numpy as np

import concourse.bass as bass
from concourse import mybir

F32 = mybir.dt.float32
F32R = mybir.dt.float32r
ALU = mybir.AluOpType
ACT = mybir.ActivationFunctionType
AX = mybir.AxisListType

P = 128
D = 2048
T = 256
KT = D // P
FF = 5632
FT = FF // P
NH = 16
PAIRS = NH // 2
KVH = 4
TOPK = min(256, T // 4)
EPS = 1e-6
ATT_SCALE = float(P) ** -0.5
WI_SCALE = float(P) ** -0.5 * float(NH) ** -0.5
BIG = 1e30
PIECE = 1024
RING = 4

QKV0 = PAIRS * 12
WO = 4 * 8
UPG = FF // 512
UP = UPG * 16
DN = 4 * (FT // 2)
L1V, L1KI, L1QI, L1K, L1Q = 8, 2, PAIRS * 4, 8, PAIRS * 4
BASE_WO = (QKV0, QKV0 + WO + UP + DN + L1V + L1KI + L1QI + L1K + L1Q)
BASE_L1 = QKV0 + WO + UP + DN
NPIECES = BASE_WO[1] + WO + UP + DN
GROUPS = 4 + 2 * UPG + 4

V_GAIN = 0
V_CONV = 4 * KT
V_DSA = V_CONV + 2 * UPG * 32
NV = V_DSA + 6
C_TRI, C_ONE, C_AVG, C_ROT, C_ID, C_SBM, C_CM, C_COS, C_SIN = 0, 128, 256, 384, 512, 640, 768, 1152, 1408
NC = 1664


def build(nc, x_in, w_all, wi_in, vecs_in, consts_in, out):
    with ExitStack() as ctx:
        def sb(name, shape, dt=F32, to=ctx):
            return to.enter_context(nc.sbuf_tensor(name, shape, dt))

        def sem(name):
            return ctx.enter_context(nc.semaphore(name))

        psum = ctx.enter_context(nc.psum_tensor("psum", [P, 8, 512], F32))

        raw = sb("raw", [P, RING, PIECE])
        w_hi = sb("w_hi", [P, RING, PIECE], F32R)
        w_lo = sb("w_lo", [P, RING, PIECE], F32R)
        xres = sb("xres", [P, KT, T])
        xg = sb("xg", [P, KT, 2 * T], F32R)
        vecs = sb("vecs", [P, NV + 1])
        avg_d = sb("avg_d", [P, P])
        rs = sb("rs", [P, T + 2])
        part = sb("part", [P, 4, T])
        upad = sb("upad", [P, 4, T + 2])
        conv = sb("conv", [P, 4, T])
        gates = sb("gates", [P, 4, T])

        with ExitStack() as mlp:
            hid = sb("hid", [P, FT, 2 * T], F32R, mlp)
        att_ctx = ctx.enter_context(ExitStack())
        att = sb("att", [P, NH, 2 * T], F32R, att_ctx)
        cst = sb("cst", [P, NC], F32, att_ctx)
        idr = sb("idr", [P, P], F32R, att_ctx)
        with ExitStack() as l0:
            sbm_r = sb("sbm_r", [P, P], F32R, l0)
            rsq = sb("rsq", [P, T], F32, l0)
            tq = sb("tq", [P, 2, T], F32, l0)
            tk = sb("tk", [P, 2, T], F32, l0)
            q0 = sb("q0", [P, 2, T], F32, l0)
            k0 = sb("k0", [P, 2, T], F32, l0)
            v0 = sb("v0", [P, 2, T], F32, l0)
            az = sb("az", [P, 2, 384], F32, l0)
            sp = sb("sp", [P, 2, 384], F32, l0)
            aw = sb("aw", [P, 2, 384], F32, l0)
        l1 = att_ctx
        v_all = sb("v_all", [P, 2, 512], F32, l1)
        v_cur = sb("v_cur", [P, 2, P], F32, l1)
        k_all = sb("k_all", [P, KVH, T], F32, l1)
        ki = sb("ki", [P, T], F32, l1)
        tu = sb("tu", [P, 2, T], F32, l1)
        usq = sb("usq", [P, 2, T], F32, l1)
        rsn = sb("rsn", [P, 2, T], F32, l1)
        ra = sb("ra", [P, 2, T], F32, l1)
        rb = sb("rb", [P, 2, T], F32, l1)
        qr = sb("qr", [P, 2, T], F32, l1)
        rl = sb("rl", [P, 2, 384], F32, l1)
        score = sb("score", [P, 384], F32, l1)
        work = sb("work", [P, 384], F32, l1)
        cum = sb("cum", [P, 384], F32, l1)
        ones = sb("ones", [P, 256], F32, l1)
        top8 = sb("top8", [P, 2, 8], F32, l1)
        tk_n = sb("tk_n", [P, 2, 2], F32, l1)
        selm = sb("selm", [P, 384], F32R, l1)
        pr = sb("pr", [P, 2, 384], F32, l1)
        prt = sb("prt", [P, 2, 384], F32, l1)
        mx = sb("mx", [P, 2, 2], F32, l1)
        nmx = sb("nmx", [P, 2, 2], F32, l1)
        sums = sb("sums", [P, 2, 2], F32, l1)
        rc = sb("rc", [P, 2, 2], F32, l1)
        rope_c = sb("rope_c", [P, 3, T], F32, l1)
        rope_s = sb("rope_s", [P, 3, T], F32, l1)
        wi_raw = sb("wi_raw", [P, KT, NH], F32, l1)
        wi_hi = sb("wi_hi", [P, KT, NH], F32R, l1)
        wi_lo = sb("wi_lo", [P, KT, NH], F32R, l1)
        wi_s = sb("wi_s", [P, 2, NH], F32, l1)
        rcs = sb("rcs", [P, 2], F32, l1)

        raw_full = [sem(f"raw_full{s}") for s in range(RING)]
        hi_ready, lo_ready, piece_used = sem("hi_ready"), sem("lo_ready"), sem("piece_used")
        vecs_in_s, avg_in, cst_in, wi_in_s = sem("vecs_loaded"), sem("avg_loaded"), sem("cst_loaded"), sem("wi_loaded")
        x_loaded = [sem(f"x_loaded{g}") for g in range(4)]
        stored, pads_zero, ones_set = sem("stored"), sem("pads_zero"), sem("ones_set")
        acc_free, b_copied = sem("acc_free"), sem("b_copied")
        x_ready, sq_ready, sqsum_ready = sem("x_ready"), sem("sq_ready"), sem("sqsum_ready")
        xhi_ready, xg_ready = sem("xhi_ready"), sem("xg_ready")
        stat_ready, root_ready, rs_ready = sem("stat_ready"), sem("root_ready"), sem("rs_ready")
        rsq_ready, id_ready = sem("rsq_ready"), sem("id_ready")
        ub_copied, up_scaled, tap0, tap1, tap2 = sem("ub_copied"), sem("up_scaled"), sem("tap0"), sem("tap1"), sem("tap2")
        silu_ready, gated, h_hi, h_ready = sem("silu_ready"), sem("gated"), sem("h_hi"), sem("h_ready")
        up_sum = sem("up_sum")
        qb_copied, kb_copied, q_sum, k_sum = sem("qb_copied"), sem("kb_copied"), sem("q_sum"), sem("k_sum")
        q_ready, k_ready, v_ready = sem("q_ready"), sem("k_ready"), sem("v_ready")
        z_ready, az_ready, e_ready, l_ready, sp_ready = (sem(n) for n in ("z_ready", "az_ready", "e_ready", "l_ready", "sp_ready"))
        la_ready, a_ready, o_ready = sem("la_ready"), sem("a_ready"), sem("o_ready")
        att_hi, att_ready = sem("att_hi"), sem("att_ready")
        v1_ready, vcur_ready = sem("v1_ready"), sem("vcur_ready")
        tables_ready = sem("tables_ready")
        wi_hi_s, wi_lo_s, wi_acc, rcs_s, wis_ready = (sem(n) for n in ("wi_hi_s", "wi_lo_s", "wi_acc", "rcs_s", "wis_ready"))
        rb_copied, rb_sum, rb_u, rb_sq = sem("rb_copied"), sem("rb_sum"), sem("rb_u"), sem("rb_sq")
        rot_ready, ms_ready, ln_ready, rsn_ready = sem("rot_ready"), sem("ms_ready"), sem("ln_ready"), sem("rsn_ready")
        terms, roped, qr_ready = sem("terms"), sem("roped"), sem("qr_ready")
        lg_ready, rl_ready, sc_half, sc_ready = sem("lg_ready"), sem("rl_ready"), sem("sc_half"), sem("sc_ready")
        topk_s, sel_ready = sem("topk_step"), sem("sel_ready")
        s_ready, mx_ready, nm_ready, p_ready, rc_ready, pn_ready = (sem(n) for n in ("s_ready", "mx_ready", "nm_ready", "p_ready", "rc_ready", "pn_ready"))
        tr_ready, pt_ready, av_ready = sem("tr_ready"), sem("pt_ready"), sem("av_ready")

        wg = w_all.rearrange("n p k -> p n k")
        tri, neg_one = cst[:, C_TRI:C_TRI + P], cst[:, C_ONE:C_ONE + P]
        avg_h, rot, ident = cst[:, C_AVG:C_AVG + P], cst[:, C_ROT:C_ROT + P], cst[:, C_ID:C_ID + P]
        cmask = cst[:, C_CM:C_CM + 384]
        cos_t, sin_t = cst[:, C_COS:C_COS + T], cst[:, C_SIN:C_SIN + T]
        at, width = (0, 128), (128, 256)

        def f32(ap):
            return ap.bitcast(F32)

        def gain(m, tile):
            return vecs[:, bass.ds(V_GAIN + m * KT + tile, 1)]

        def times(i, n):
            return 0 if i is None else i * n

        block = ctx.enter_context(nc.Block())

        @block.sync
        def _(sp_q):
            for n in range(RING):
                sp_q.dma_start(raw[:, n, :], wg[:, n, :]).then_inc(raw_full[n], 16)
            loops = (NPIECES - RING) // RING
            with sp_q.Fori(0, loops) as i:
                for s in range(RING):
                    sp_q.wait_ge(lo_ready, i * RING + s + 1)
                    sp_q.dma_start(raw[:, s, :], wg[:, bass.ds(i * RING + RING + s, 1), :]).then_inc(raw_full[s], 16)
            for n in range(RING * (loops + 1), NPIECES):
                sp_q.wait_ge(lo_ready, n - RING + 1)
                sp_q.dma_start(raw[:, n % RING, :], wg[:, n, :]).then_inc(raw_full[n % RING], 16)

        @block.gpsimd
        def _(pool):
            pool.memset(upad[:, :, 0:2], 0.0).then_inc(pads_zero, 1)
            for g in range(4):
                pool.wait_ge(x_ready, 12 + g + 1)
                pool.dma_start(out[:, 4 * g:4 * g + 4, :], xres[:, 4 * g:4 * g + 4, :]).then_inc(stored, 16)
            pool.wait_ge(stored, 64)

        @block.scalar
        def _(act):
            def split(c, i=None, per=0):
                if c >= NPIECES:
                    return
                act.wait_ge(raw_full[c % RING], times(i, 16 * per // RING) + 16 * (c // RING + 1))
                if c >= RING or i is not None:
                    act.wait_ge(piece_used, times(i, per) + c - RING + 1)
                act.copy(w_hi[:, c % RING, :], raw[:, c % RING, :]).then_inc(hi_ready, 1)

            def norm(m, g):
                n = 4 * m + g
                if m == 0:
                    act.wait_ge(x_loaded[g], 16)
                else:
                    act.wait_ge(x_ready, n - 4 + 1)
                if not (m == 0 and g == 0):
                    act.wait_ge(sqsum_ready, n)
                act.activation(conv[:, :, :], xres[:, bass.ds(4 * g, 4), :], ACT.Square).then_inc(sq_ready, 1)
                for k in range(4):
                    last = act.activation(xg[:, 4 * g + k, 0:T], xres[:, 4 * g + k, :], ACT.Copy, scale=gain(m, 4 * g + k))
                last.then_inc(xhi_ready, 1)

            def root(m, bank):
                act.wait_ge(stat_ready, m + 1)
                act.activation(rs[:, :], psum[:, bank, 0:T + 2], ACT.Sqrt, bias=eps_ap).then_inc(root_ready, 1)

            def copy_b(group, bank0, last_piece):
                act.wait_ge(piece_used, last_piece + 1)
                act.wait_ge(x_ready, group) if group else None
                act.copy(part[:, :, :], psum[:, bank0:bank0 + 4, T:2 * T]).then_inc(b_copied, 1)

            def out_groups(base, layer, per, m, tail=None):
                for g in range(4):
                    for e in range(per):
                        c = base + g * per + e
                        split(c + RING)
                        if tail and g == 0:
                            tail(e)
                    copy_b(outg(layer, m) + g, 4 * (g % 2), base + g * per + per - 1)
                    if m < 4:
                        norm(m, g)

            def outg(layer, m):
                return {1: 0, 2: 4, 3: 8, 4: 12}[m]

            eps_ap = vecs[:, NV:NV + 1]

            act.dma_start(xres[:, 0:4, :], x_in[:, 0:4, :]).then_inc(x_loaded[0], 16)
            act.dma_start(vecs[:, :], vecs_in).then_inc(vecs_in_s, 16)
            for g in range(1, 4):
                act.dma_start(xres[:, 4 * g:4 * g + 4, :], x_in[:, 4 * g:4 * g + 4, :]).then_inc(x_loaded[g], 16)
            act.dma_start(avg_d[:, :], consts_in[:, NC:NC + P]).then_inc(avg_in, 16)
            act.dma_start(cst[:, :], consts_in[:, 0:NC]).then_inc(cst_in, 16)
            act.wait_ge(vecs_in_s, 16)
            for g in range(4):
                norm(0, g)
                split(g)

            def l0_ab(j):
                act.wait_ge(la_ready, j + 1)
                if not isinstance(j, int) or j > 0:
                    act.wait_ge(o_ready, j)
                act.activation(aw[:, :, :], psum[:, 5:7, 0:384], ACT.Exp).then_inc(a_ready, 1)

            def l0_out(j):
                act.wait_ge(o_ready, j + 1)
                act.copy(att[:, bass.ds(2 * j, 2), 0:T], psum[:, 7, :].rearrange("p (h t) -> p h t", h=2)).then_inc(att_hi, 1)

            def l0_pair(j, i, per, first):
                for e in range(12):
                    split((0 if i is not None else 0) + e + RING + (0 if i is not None else 12 * j), i, per)
                    n0 = 12 * j
                    if e == 0 and not first:
                        l0_ab(j - 1)
                    if e == 2 and first:
                        root(0, 7)
                    if e == 2 and not first:
                        l0_out(j - 1)
                    if e == 3:
                        act.wait_ge(piece_used, n0 + 4)
                        if not first:
                            act.wait_ge(q_ready, j)
                        act.copy(tq[:, :, :], psum[:, 0:2, T:2 * T]).then_inc(qb_copied, 1)
                    if e == 7:
                        act.wait_ge(piece_used, n0 + 8)
                        if not first:
                            act.wait_ge(k_ready, j)
                        act.copy(tk[:, :, :], psum[:, 2:4, T:2 * T]).then_inc(kb_copied, 1)
                    if e == 9:
                        act.wait_ge(z_ready, j + 1)
                        if not first:
                            act.wait_ge(sp_ready, j)
                        act.activation(az[:, :, :], psum[:, 5:7, 0:384], ACT.Abs).then_inc(az_ready, 1)
                        act.wait_ge(az_ready, j + 1)
                        act.activation(az[:, :, :], az[:, :, :], ACT.Exp, scale=-1.0).then_inc(e_ready, 1)
                        act.wait_ge(e_ready, j + 1)
                        act.activation(az[:, :, :], az[:, :, :], ACT.Ln, bias=1.0).then_inc(l_ready, 1)
                    if e == 11:
                        act.wait_ge(piece_used, n0 + 12)
                        if not first:
                            act.wait_ge(o_ready, j)
                        act.wait_ge(rs_ready, 1)
                        for st in range(2):
                            last = act.activation(v0[:, st, :], psum[:, 4, st * T:(st + 1) * T], ACT.Copy, scale=rs[:, T + st:T + st + 1])
                        last.then_inc(v_ready, 1)

            act.wait_ge(cst_in, 16)
            act.copy(idr[:, :], ident)
            act.copy(sbm_r[:, :], cst[:, C_SBM:C_SBM + P]).then_inc(id_ready, 1)
            l0_pair(0, None, 0, True)
            with act.Fori(1, PAIRS) as i:
                l0_pair(i, i, 12, False)

            def l0_tail(e):
                if e == 0:
                    l0_ab(PAIRS - 1)
                if e == 2:
                    l0_out(PAIRS - 1)
            out_groups(BASE_WO[0], 0, 8, 1, l0_tail)

            def conv_scalars(layer, i, val, k, j):
                return vecs[:, bass.ds(V_CONV + layer * UPG * 32 + times(i, 32) + val * 16 + k * 4 + j, 1)]

            def up_group(layer, i, val, last_piece):
                u = 2 * UPG * layer + 2 * i + val
                f = UPG * layer + i
                act.wait_ge(piece_used, last_piece + 1)
                act.copy(part[:, :, :], psum[:, 4 * val:4 * val + 4, T:2 * T]).then_inc(ub_copied, 1)
                act.wait_ge(up_scaled, u + 1)
                if not val and not (isinstance(f, int) and f == 0):
                    act.wait_ge(gated, f)
                for k in range(4):
                    last = act.activation(conv[:, k, :], upad[:, k, 0:T], ACT.Identity,
                                          scale=conv_scalars(layer, i, val, k, 0), bias=conv_scalars(layer, i, val, k, 3))
                last.then_inc(tap0, 1)
                if not val:
                    act.wait_ge(tap2, u + 1)
                    if not (isinstance(f, int) and f == 0):
                        act.wait_ge(h_ready, f)
                    act.activation(gates[:, :, :], conv[:, :, :], ACT.Silu).then_inc(silu_ready, 1)
                else:
                    act.wait_ge(gated, f + 1)
                    act.copy(hid[:, bass.ds(4 * i, 4), 0:T], gates[:, :, :]).then_inc(h_hi, 1)

            def up_body(layer, i, fi, base, m):
                for e in range(16):
                    split(base + e + RING, fi, 16)
                    if m is not None and e == 4:
                        root(m, 4)
                    if e == 7:
                        up_group(layer, i, 0, base + 16 * i + 7)
                    if e == 15:
                        up_group(layer, i, 1, base + 16 * i + 15)

            def mlp_layer(layer):
                base = BASE_WO[layer] + WO
                up_body(layer, 0, None, base, 1 + 2 * layer)
                with act.Fori(1, UPG) as i:
                    up_body(layer, i, i, base, None)

            mlp_layer(0)

            def down(layer):
                base = BASE_WO[layer] + WO + UP
                m = 2 if layer == 0 else 4
                out_groups(base, layer, FT // 2, m)
            down(0)

            act.dma_start(cst[:, :], consts_in[:, 0:NC]).then_inc(cst_in, 16)
            act.dma_start(wi_raw[:, :, :], wi_in).then_inc(wi_in_s, 16)
            for e in range(8):
                split(BASE_L1 + e + RING)
                if e == 0:
                    act.wait_ge(cst_in, 32)
                    act.copy(idr[:, :], ident).then_inc(id_ready, 1)
                    act.wait_ge(wi_in_s, 16)
                    act.copy(wi_hi[:, :, :], wi_raw[:, :, :]).then_inc(wi_hi_s, 1)
                if e == 4:
                    root(2, 4)
                if e == 7:
                    act.wait_ge(piece_used, BASE_L1 + 8)
                    act.wait_ge(rs_ready, 3)
                    for st in range(2):
                        last = act.activation(v_all[:, st, :], psum[:, st, :], ACT.Copy, scale=rs[:, T + st:T + st + 1])
                    last.then_inc(v1_ready, 1)

            def evac(B, bank0, nh, last_piece, nb):
                act.wait_ge(piece_used, last_piece + 1)
                if not (isinstance(B, int) and B == 0):
                    act.wait_ge(qr_ready, B)
                act.copy(tu[:, 0:nh, :], psum[:, bank0:bank0 + nh, T:2 * T]).then_inc(rb_copied, 1)
                if nb is not None:
                    act.wait_ge(rb_u, nb + 1)
                    act.activation(usq[:, 0:nh, :], tu[:, 0:nh, :], ACT.Square).then_inc(rb_sq, 1)

            def norm_scale(nh, nb):
                act.wait_ge(ms_ready, nb + 1)
                act.activation(rsn[:, 0:nh, :], psum[:, 5, 0:nh * T].rearrange("p (h t) -> p h t", h=nh), ACT.Ln, bias=eps_ap).then_inc(ln_ready, 1)
                act.wait_ge(ln_ready, nb + 1)
                act.activation(rsn[:, 0:nh, :], rsn[:, 0:nh, :], ACT.Exp, scale=-0.5).then_inc(rsn_ready, 1)

            def relu(t):
                act.wait_ge(lg_ready, t + 1)
                if not (isinstance(t, int) and t == 0):
                    act.wait_ge(sc_ready, t)
                act.activation(rl[:, :, :], psum[:, 6:8, 0:384], ACT.Relu).then_inc(rl_ready, 1)

            def exps(t):
                act.wait_ge(nm_ready, t + 1)
                if not (isinstance(t, int) and t == 0):
                    act.wait_ge(tr_ready, t)
                for h in range(2):
                    for th in range(2):
                        c = slice(at[th], at[th] + width[th])
                        last = act.activation(pr[:, h, c], psum[:, 6 + h, c], ACT.Exp, bias=nmx[:, th, h:h + 1], scale=ATT_SCALE,
                                              accum_out=sums[:, th, h:h + 1])
                last.then_inc(p_ready, 1)

            def prt_copy(t):
                act.wait_ge(tr_ready, t + 1)
                if not (isinstance(t, int) and t == 0):
                    act.wait_ge(av_ready, t)
                act.copy(prt[:, :, :], psum[:, 6:8, 0:384]).then_inc(pt_ready, 1)

            def out_hi(t):
                act.wait_ge(av_ready, t + 1)
                act.copy(att[:, bass.ds(2 * t, 2), 0:T], psum[:, 4, :].rearrange("p (h t) -> p h t", h=2)).then_inc(att_hi, 1)

            def set_v(g):
                if not (isinstance(g, int) and g == 0):
                    act.wait_ge(av_ready, 2 * g)
                act.copy(v_cur[:, :, :], v_all[:, :, bass.ds(g * P, P)]).then_inc(vcur_ready, 1)

            kbase = BASE_L1 + L1V
            for e in range(2):
                split(kbase + e + RING)
            evac(0, 2, 1, kbase + 1, 0)
            qibase = kbase + L1KI

            def block1(B, i, per, par, nb, prev_norm, t_relu, t_soft, t_av, base, v_g=None):
                for e in range(4):
                    split(base + e + RING, i, per)
                    if e == 0 and t_relu is not None:
                        relu(t_relu)
                    if e == 0 and v_g is not None:
                        set_v(v_g)
                    if e == 0 and t_soft is not None:
                        exps(t_soft)
                    if e == 1 and prev_norm is not None:
                        norm_scale(prev_norm[1], prev_norm[0])
                    if e == 2 and t_soft is not None:
                        prt_copy(t_soft)
                    if e == 3:
                        evac(B, 2 * par, 2, base + times(i, per) + 3, nb)
                        if t_av is not None:
                            out_hi(t_av)

            block1(1, None, 0, 0, None, (0, 1), None, None, None, qibase)
            block1(2, None, 0, 1, None, None, None, None, None, qibase + 4)
            with act.Fori(0, 3) as i:
                block1(3 + 2 * i, i, 8, 0, None, None, 2 * i, None, None, qibase + 8)
                block1(4 + 2 * i, i, 8, 1, None, None, 2 * i + 1, None, None, qibase + 12)
            block1(9, None, 0, 0, 1, None, 6, None, None, qibase + 32)
            block1(10, None, 0, 1, 2, (1, 2), 7, None, None, qibase + 36)
            block1(11, None, 0, 0, 3, (2, 2), None, None, None, qibase + 40)
            block1(12, None, 0, 1, 4, (3, 2), None, None, None, qibase + 44)
            with act.Fori(0, 3) as i:
                block1(13 + 2 * i, i, 8, 0, 5 + 2 * i, (4 + 2 * i, 2), None, 2 * i, 2 * i, qibase + 48, v_g=i)
                block1(14 + 2 * i, i, 8, 1, 6 + 2 * i, (5 + 2 * i, 2), None, 2 * i + 1, 2 * i + 1, qibase + 52)

            def l1_tail(e):
                if e == 0:
                    set_v(3)
                    exps(6)
                if e == 1:
                    norm_scale(2, 10)
                if e == 2:
                    prt_copy(6)
                if e == 3:
                    out_hi(6)
                if e == 4:
                    exps(7)
                if e == 6:
                    prt_copy(7)
                    out_hi(7)
            out_groups(BASE_WO[1], 1, 8, 3, l1_tail)
            mlp_layer(1)
            down(1)

        @block.vector
        def _(dve):
            def split(c, i=None, per=0):
                if c >= NPIECES:
                    return
                dve.wait_ge(hi_ready, times(i, per) + c + 1)
                dve.tensor_tensor(w_lo[:, c % RING, :], raw[:, c % RING, :], f32(w_hi[:, c % RING, :]), ALU.subtract).then_inc(lo_ready, 1)

            def norm(m, g):
                n = 4 * m + g
                dve.wait_ge(sq_ready, n + 1)
                dve.tensor_reduce(gates[:, g, :], conv[:, :, :].rearrange("p k t -> p t k"), AX.X, ALU.add).then_inc(sqsum_ready, 1)
                dve.wait_ge(xhi_ready, n + 1)
                for k in range(4):
                    last = dve.scalar_tensor_tensor(out=xg[:, 4 * g + k, T:2 * T], in0=xres[:, 4 * g + k, :], scalar=gain(m, 4 * g + k),
                                                    in1=f32(xg[:, 4 * g + k, 0:T]), op0=ALU.mult, op1=ALU.subtract)
                last.then_inc(xg_ready, 1)

            def recip(m):
                dve.wait_ge(root_ready, m + 1)
                dve.reciprocal(rs[:, :], rs[:, :]).then_inc(rs_ready, 1)

            def add_group(o, g, bank0):
                dve.wait_ge(b_copied, o + 1)
                dve.tensor_tensor(part[:, :, :], psum[:, bank0:bank0 + 4, 0:T], part[:, :, :], ALU.add).then_inc(acc_free, 1)
                dve.wait_ge(acc_free, GROUPS * (o // 8) + (4 + 2 * UPG) * (o // 4 % 2) + g + 1)
                dve.tensor_tensor(xres[:, 4 * g:4 * g + 4, :], xres[:, 4 * g:4 * g + 4, :], part[:, :, :], ALU.add).then_inc(x_ready, 1)

            def out_groups(base, per, m, o, tail=None):
                for g in range(4):
                    for e in range(per):
                        split(base + g * per + e + RING)
                        if tail and g == 0:
                            tail(e)
                    add_group(o + g, g, 4 * (g % 2))
                    if m < 4:
                        norm(m, g)

            dve.wait_ge(vecs_in_s, 16)
            for g in range(4):
                dve.wait_ge(x_loaded[g], 16)
                norm(0, g)
                split(g)

            def l0_out(j):
                dve.wait_ge(att_hi, j + 1)
                dst = att[:, bass.ds(2 * j, 2), :]
                dve.tensor_tensor(dst[:, :, T:2 * T], psum[:, 7, :].rearrange("p (h t) -> p h t", h=2), f32(dst[:, :, 0:T]),
                                  ALU.subtract).then_inc(att_ready, 1)

            def over_heads(ap, n=2):
                return ap.unsqueeze(1).to_broadcast([P, n, T])

            def l0_pair(j, i, per, first):
                n0 = None if i is not None else 12 * j
                for e in range(12):
                    split((0 if i is not None else 12 * j) + e + RING, i, per)
                    if e == 2 and first:
                        recip(0)
                        dve.wait_ge(rs_ready, 1)
                        dve.tensor_scalar(rsq[:, :], rs[:, 0:T], ATT_SCALE, None, ALU.mult).then_inc(rsq_ready, 1)
                        dve.wait_ge(rsq_ready, 1)
                    if e == 2 and not first:
                        l0_out(j - 1)
                    for at_e, b_done, tmp, summed, scale, dst, done, bank in (
                            (3, qb_copied, tq, q_sum, rsq[:, :], q0, q_ready, 0), (7, kb_copied, tk, k_sum, rs[:, 0:T], k0, k_ready, 2)):
                        if e == at_e:
                            dve.wait_ge(b_done, j + 1)
                            dve.tensor_tensor(tmp[:, :, :], psum[:, bank:bank + 2, 0:T], tmp[:, :, :], ALU.add).then_inc(summed, 1)
                            dve.wait_ge(summed, j + 1)
                            if not first:
                                dve.wait_ge(z_ready, j)
                            dve.tensor_tensor(dst[:, :, :], tmp[:, :, :], over_heads(scale), ALU.mult).then_inc(done, 1)
                    if e == 10:
                        dve.wait_ge(l_ready, j + 1)
                        if not first:
                            dve.wait_ge(la_ready, j)
                        dve.scalar_tensor_tensor(out=sp[:, :, :], in0=psum[:, 5:7, 0:384], scalar=0.0, in1=az[:, :, :],
                                                 op0=ALU.max, op1=ALU.add).then_inc(sp_ready, 1)

            l0_pair(0, None, 0, True)
            with dve.Fori(1, PAIRS) as i:
                l0_pair(i, i, 12, False)

            def l0_tail(e):
                if e == 2:
                    l0_out(PAIRS - 1)
            out_groups(BASE_WO[0], 8, 1, 0, l0_tail)

            def conv_scalars(layer, i, val, k, j):
                return vecs[:, bass.ds(V_CONV + layer * UPG * 32 + times(i, 32) + val * 16 + k * 4 + j, 1)]

            def up_group(layer, i, val):
                u = 2 * UPG * layer + 2 * i + val
                f = UPG * layer + i
                n = GROUPS * layer + 4 + 2 * i + val
                dve.wait_ge(ub_copied, u + 1)
                dve.tensor_tensor(part[:, :, :], psum[:, 4 * val:4 * val + 4, 0:T], part[:, :, :], ALU.add).then_inc(acc_free, 1)
                dve.wait_ge(acc_free, n + 1)
                dve.tensor_tensor(upad[:, :, 2:T + 2], part[:, :, :], over_heads(rs[:, 0:T], 4), ALU.mult).then_inc(up_scaled, 1)
                dve.wait_ge(tap0, u + 1)
                for j, done in ((1, tap1), (2, tap2)):
                    for k in range(4):
                        last = dve.scalar_tensor_tensor(out=conv[:, k, :], in0=upad[:, k, j:j + T], scalar=conv_scalars(layer, i, val, k, j),
                                                        in1=conv[:, k, :], op0=ALU.mult, op1=ALU.add)
                    last.then_inc(done, 1)
                    dve.wait_ge(done, u + 1)
                if val:
                    dve.wait_ge(silu_ready, f + 1)
                    dve.tensor_tensor(gates[:, :, :], gates[:, :, :], conv[:, :, :], ALU.mult).then_inc(gated, 1)
                    dve.wait_ge(h_hi, f + 1)
                    dst = hid[:, bass.ds(4 * i, 4), :]
                    dve.tensor_tensor(dst[:, :, T:2 * T], gates[:, :, :], f32(dst[:, :, 0:T]), ALU.subtract).then_inc(h_ready, 1)

            def up_body(layer, i, fi, base, m):
                for e in range(16):
                    split(base + e + RING, fi, 16)
                    if m is not None and e == 4:
                        recip(m)
                        dve.wait_ge(rs_ready, m + 1)
                    if e == 7:
                        up_group(layer, i, 0)
                    if e == 15:
                        up_group(layer, i, 1)

            def mlp_layer(layer):
                base = BASE_WO[layer] + WO
                if layer == 0:
                    dve.wait_ge(pads_zero, 1)
                up_body(layer, 0, None, base, 1 + 2 * layer)
                with dve.Fori(1, UPG) as i:
                    up_body(layer, i, i, base, None)

            mlp_layer(0)
            out_groups(BASE_WO[0] + WO + UP, FT // 2, 2, 4)

            for e in range(8):
                split(BASE_L1 + e + RING)
                if e == 1:
                    dve.wait_ge(cst_in, 32)
                    for n in range(3):
                        dve.tensor_scalar(rope_c[:, n, :], cos_t, vecs[:, V_DSA + n:V_DSA + n + 1], None, ALU.mult)
                        last = dve.tensor_scalar(rope_s[:, n, :], sin_t, vecs[:, V_DSA + 3 + n:V_DSA + 4 + n], None, ALU.mult)
                    last.then_inc(tables_ready, 1)
                    dve.memset(score[:, :], 0.0)
                    dve.memset(ones[:, :], 1.0).then_inc(ones_set, 1)
                    dve.wait_ge(ones_set, 1)
                    dve.wait_ge(wi_hi_s, 1)
                    dve.tensor_tensor(wi_lo[:, :, :], wi_raw[:, :, :], f32(wi_hi[:, :, :]), ALU.subtract).then_inc(wi_lo_s, 1)
                    dve.wait_ge(tables_ready, 1)
                if e == 4:
                    recip(2)
                    dve.wait_ge(rs_ready, 3)
                    dve.tensor_scalar(rcs[:, :], rs[:, T:T + 2], WI_SCALE, None, ALU.mult).then_inc(rcs_s, 1)

            def evac(B, bank0, nh, nb):
                dve.wait_ge(rb_copied, B + 1)
                dve.tensor_tensor(tu[:, 0:nh, :], psum[:, bank0:bank0 + nh, 0:T], tu[:, 0:nh, :], ALU.add).then_inc(rb_sum, 1)
                if nb is not None:
                    dve.wait_ge(rb_sum, B + 1)
                    dve.tensor_tensor(tu[:, 0:nh, :], tu[:, 0:nh, :], over_heads(rs[:, 0:T], nh), ALU.mult).then_inc(rb_u, 1)

            def rope(B, nh, nb, c_t, s_t, dst, after=None):
                dve.wait_ge(rot_ready, B + 1)
                dve.tensor_tensor(ra[:, 0:nh, :], tu[:, 0:nh, :], over_heads(c_t, nh), ALU.mult)
                dve.tensor_tensor(rb[:, 0:nh, :], psum[:, 4, 0:nh * T].rearrange("p (h t) -> p h t", h=nh), over_heads(s_t, nh),
                                  ALU.mult).then_inc(terms, 1)
                dve.wait_ge(terms, B + 1)
                if after is not None:
                    dve.wait_ge(*after)
                if nb is None:
                    dve.tensor_tensor(dst, ra[:, 0:nh, :], rb[:, 0:nh, :], ALU.add).then_inc(qr_ready, 1)
                else:
                    dve.tensor_tensor(ra[:, 0:nh, :], ra[:, 0:nh, :], rb[:, 0:nh, :], ALU.add).then_inc(roped, 1)
                    dve.wait_ge(roped, nb + 1)
                    dve.wait_ge(rsn_ready, nb + 1)
                    dve.tensor_tensor(dst, ra[:, 0:nh, :], rsn[:, 0:nh, :], ALU.mult).then_inc(qr_ready, 1)

            def rope_prev(B, kind, nb=None):
                if kind == "ki":
                    rope(B, 1, nb, rope_c[:, 2, :], rope_s[:, 2, :], ki[:, :].unsqueeze(1))
                elif kind == "qi":
                    first = isinstance(B, int) and B == 1
                    rope(B, 2, None, cos_t, sin_t, qr[:, :, :], None if first else (lg_ready, B - 1))
                elif kind == "k":
                    rope(B, 2, nb, rope_c[:, 1, :], rope_s[:, 1, :], k_all[:, 2 * (B - 9):2 * (B - 9) + 2, :])
                else:
                    after = (lg_ready, 8) if isinstance(B, int) and B == 11 else (s_ready, B - 11)
                    rope(B, 2, nb, rope_c[:, 0, :], rope_s[:, 0, :], qr[:, :, :], after)

            def add_scores(t):
                dve.wait_ge(rl_ready, t + 1)
                if isinstance(t, int) and t == 0:
                    dve.wait_ge(wis_ready, 1)
                for h in range(2):
                    if h or not (isinstance(t, int) and t == 0):
                        dve.wait_ge(sc_half if h else sc_ready, t + h)
                    for th in range(2):
                        c = slice(at[th], at[th] + width[th])
                        last = dve.scalar_tensor_tensor(out=score[:, c], in0=rl[:, h, c], scalar=wi_s[:, th, bass.ds(2 * t + h, 1)],
                                                        in1=score[:, c], op0=ALU.mult, op1=ALU.add)
                    last.then_inc(sc_ready if h else sc_half, 1)

            step = [0]

            def link(ins):
                step[0] += 1
                ins.then_inc(topk_s, 1)
                dve.wait_ge(topk_s, step[0])

            def mask_scores():
                dve.wait_ge(sc_ready, PAIRS)
                link(dve.tensor_tensor(score[:, :], score[:, :], cmask, ALU.add))
                link(dve.tensor_copy(work[:, :], score[:, :]))

            def top_rounds(th, lo, hi):
                w = work[:, at[th]:at[th] + width[th]]
                for r in range(lo, hi):
                    link(dve.max(top8[:, th, :], w))
                    if r < TOPK // 8 - 1:
                        link(dve.match_replace(w, top8[:, th, :], w, -3e38))

            def select(th):
                c = slice(at[th], at[th] + width[th])
                thr = top8[:, th, 7:8]
                link(dve.tensor_scalar(work[:, c], score[:, c], thr, None, ALU.is_gt))
                link(dve.tensor_reduce(tk_n[:, th, 0:1], work[:, c], AX.X, ALU.add))
                link(dve.tensor_scalar(tk_n[:, th, 1:2], tk_n[:, th, 0:1], -1.0, float(TOPK), ALU.mult, ALU.add))
                link(dve.tensor_scalar(score[:, c], score[:, c], thr, None, ALU.is_equal))
                link(dve.tensor_tensor_scan(cum[:, c], ones[:, 0:width[th]], score[:, c], 0.0, ALU.mult, ALU.add))
                link(dve.scalar_tensor_tensor(out=score[:, c], in0=cum[:, c], scalar=tk_n[:, th, 1:2], in1=score[:, c],
                                              op0=ALU.is_le, op1=ALU.mult))
                link(dve.tensor_tensor(work[:, c], work[:, c], score[:, c], ALU.add))
                link(dve.tensor_scalar(work[:, c], work[:, c], -1.0, BIG, ALU.add, ALU.mult))
                dve.tensor_tensor(selm[:, c], work[:, c], cmask[:, c], ALU.add).then_inc(sel_ready, 1)

            def maxes(t):
                dve.wait_ge(s_ready, t + 1)
                for th in range(2):
                    last = dve.tensor_reduce(mx[:, th, :], psum[:, 6:8, at[th]:at[th] + width[th]], AX.X, ALU.max)
                last.then_inc(mx_ready, 1)
                dve.wait_ge(mx_ready, t + 1)
                dve.tensor_scalar(nmx[:, :, :], mx[:, :, :], -ATT_SCALE, None, ALU.mult).then_inc(nm_ready, 1)

            def normalise(t):
                dve.wait_ge(p_ready, t + 1)
                dve.reciprocal(rc[:, :, :], sums[:, :, :]).then_inc(rc_ready, 1)
                dve.wait_ge(rc_ready, t + 1)
                for h in range(2):
                    for th in range(2):
                        c = slice(at[th], at[th] + width[th])
                        last = dve.tensor_scalar(pr[:, h, c], pr[:, h, c], rc[:, th, h:h + 1], None, ALU.mult)
                last.then_inc(pn_ready, 1)

            def out_lo(t):
                dve.wait_ge(att_hi, PAIRS + t + 1)
                dst = att[:, bass.ds(2 * t, 2), :]
                dve.tensor_tensor(dst[:, :, T:2 * T], psum[:, 4, :].rearrange("p (h t) -> p h t", h=2), f32(dst[:, :, 0:T]),
                                  ALU.subtract).then_inc(att_ready, 1)

            kbase = BASE_L1 + L1V
            for e in range(2):
                split(kbase + e + RING)
            evac(0, 2, 1, 0)
            dve.wait_ge(wi_acc, 1)
            dve.wait_ge(rcs_s, 1)
            for th in range(2):
                last = dve.tensor_scalar(wi_s[:, th, :], psum[:, 5, th * NH:(th + 1) * NH], rs[:, T + th:T + th + 1], rcs[:, th:th + 1],
                                         ALU.mult, ALU.mult)
            last.then_inc(wis_ready, 1)
            qibase = kbase + L1KI

            def block1(B, i, per, par, nb, prev, t_score, t_soft, t_av, base, extra=None):
                for e in range(4):
                    split(base + e + RING, i, per)
                    if e == 0 and t_score is not None:
                        add_scores(t_score)
                    if e == 0 and t_soft is not None:
                        maxes(t_soft)
                    if e == 1 and t_soft is not None:
                        normalise(t_soft)
                    if e == 1:
                        rope_prev(B - 1, *prev)
                    if e == 3:
                        evac(B, 2 * par, 2, nb)
                        if t_av is not None:
                            out_lo(t_av)
                    if extra is not None:
                        extra(e)

            def topk_a(e):
                if e == 0:
                    mask_scores()
                if e == 2:
                    top_rounds(1, 0, 4)

            def topk_b(e):
                if e == 0:
                    top_rounds(1, 4, 8)
                if e == 2:
                    top_rounds(0, 0, 8)

            def topk_c(e):
                if e == 0:
                    select(0)
                if e == 2:
                    select(1)

            block1(1, None, 0, 0, None, ("ki", 0), None, None, None, qibase)
            block1(2, None, 0, 1, None, ("qi",), None, None, None, qibase + 4)
            with dve.Fori(0, 3) as i:
                block1(3 + 2 * i, i, 8, 0, None, ("qi",), 2 * i, None, None, qibase + 8)
                block1(4 + 2 * i, i, 8, 1, None, ("qi",), 2 * i + 1, None, None, qibase + 12)
            block1(9, None, 0, 0, 1, ("qi",), 6, None, None, qibase + 32)
            block1(10, None, 0, 1, 2, ("k", 1), 7, None, None, qibase + 36, topk_a)
            block1(11, None, 0, 0, 3, ("k", 2), None, None, None, qibase + 40, topk_b)
            block1(12, None, 0, 1, 4, ("q", 3), None, None, None, qibase + 44, topk_c)
            with dve.Fori(0, 3) as i:
                block1(13 + 2 * i, i, 8, 0, 5 + 2 * i, ("q", 4 + 2 * i), None, 2 * i, 2 * i, qibase + 48)
                block1(14 + 2 * i, i, 8, 1, 6 + 2 * i, ("q", 5 + 2 * i), None, 2 * i + 1, 2 * i + 1, qibase + 52)

            def l1_tail(e):
                if e == 0:
                    maxes(6)
                if e == 1:
                    normalise(6)
                    rope_prev(18, "q", 10)
                if e == 3:
                    out_lo(6)
                if e == 4:
                    maxes(7)
                if e == 5:
                    normalise(7)
                if e == 6:
                    out_lo(7)
            out_groups(BASE_WO[1], 8, 3, 8, l1_tail)
            mlp_layer(1)
            out_groups(BASE_WO[1] + WO + UP, FT // 2, 4, 12)

        @block.tensor
        def _(pe):
            def mm(o, lhsT, rhs, start=False):
                return pe.matmul(o, lhsT, rhs, start=start, stop=True, skip_group_check=True)

            def proj(c, i, per, bank0, act_in, kts, k0_, cols, first):
                pe.wait_ge(lo_ready, times(i, per) + c + 1)
                s = c % RING
                for ct in range(cols // P):
                    for kk in range(kts):
                        w = slice(kk * cols + ct * P, kk * cols + (ct + 1) * P)
                        k = k0_ + kk
                        mm(psum[:, bank0 + ct, :], w_hi[:, s, w], act_in[:, k, :], first and kk == 0)
                        last = mm(psum[:, bank0 + ct, 0:T], w_lo[:, s, w], act_in[:, k, 0:T])
                last.then_inc(piece_used, 1)

            def proj_tokens(c, i, per, places, kts, k0_, cols, first):
                pe.wait_ge(lo_ready, times(i, per) + c + 1)
                s = c % RING
                for kk in range(kts):
                    w = slice(kk * cols, (kk + 1) * cols)
                    for th in range(2):
                        k = k0_ + kk
                        new = first and kk == 0 and places[th][1]
                        x_hi, x_lo = xg[:, k, th * P:(th + 1) * P], xg[:, k, T + th * P:T + (th + 1) * P]
                        mm(places[th][0], x_hi, w_hi[:, s, w], new)
                        mm(places[th][0], x_hi, w_lo[:, s, w])
                        last = mm(places[th][0], x_lo, w_hi[:, s, w])
                last.then_inc(piece_used, 1)

            def stat(m, bank):
                pe.wait_ge(sqsum_ready, 4 * (m + 1))
                if m == 0:
                    pe.wait_ge(avg_in, 16)
                for g in range(4):
                    mm(psum[:, bank, 0:T], avg_d[:, :], gates[:, g, :], g == 0)
                for th in range(2):
                    for g in range(4):
                        last = mm(psum[:, bank, T + th:T + th + 1], gates[:, g, th * P:(th + 1) * P], avg_d[:, 0:1])
                last.then_inc(stat_ready, 1)

            def out_groups(base, layer, per, src, n0, ready, tail=None):
                for g in range(4):
                    n = GROUPS * layer + n0 + g
                    if g >= 2 or n0:
                        pe.wait_ge(acc_free, n - 1)
                    for e in range(per):
                        if g == 0:
                            ready(e)
                        proj(base + g * per + e, None, 0, 4 * (g % 2), src, 2, 2 * e, 512, e == 0)
                        if tail and g == 0:
                            tail(e)

            def l0_logits(j):
                pe.wait_ge(q_ready, j + 1)
                pe.wait_ge(k_ready, j + 1)
                if not (isinstance(j, int) and j == 0):
                    pe.wait_ge(a_ready, j)
                for h in range(2):
                    b = 5 + h
                    mm(psum[:, b, 0:T], k0[:, h, 0:P], q0[:, h, :], True)
                    mm(psum[:, b, T:384], k0[:, h, P:T], q0[:, h, P:T])
                    mm(psum[:, b, 0:P], idr[:, :], sbm_r[:, :])
                    last = mm(psum[:, b, T:384], idr[:, :], sbm_r[:, :])
                last.then_inc(z_ready, 1)

            def l0_tri(j):
                pe.wait_ge(sp_ready, j + 1)
                for h in range(2):
                    b = 5 + h
                    mm(psum[:, b, 0:T], tri, sp[:, h, 0:T])
                    mm(psum[:, b, P:T], neg_one, sp[:, h, T:384])
                    last = mm(psum[:, b, T:384], tri, sp[:, h, T:384])
                last.then_inc(la_ready, 1)

            def l0_av(j):
                pe.wait_ge(a_ready, j + 1)
                pe.wait_ge(v_ready, j + 1)
                if not (isinstance(j, int) and j == 0):
                    pe.wait_ge(att_ready, j)
                for h in range(2):
                    mm(psum[:, 7, h * T:(h + 1) * T], v0[:, 0, h * P:(h + 1) * P], aw[:, h, 0:T], h == 0)
                    last = mm(psum[:, 7, h * T + P:(h + 1) * T], v0[:, 1, h * P:(h + 1) * P], aw[:, h, T:384])
                last.then_inc(o_ready, 1)

            def l0_pair(j, i, per, first):
                c0 = 0 if i is not None else 12 * j
                for e in range(12):
                    kind, q = e // 4, e % 4
                    if first and kind == 0:
                        pe.wait_ge(xg_ready, q + 1)
                    if q == 0 and not first:
                        pe.wait_ge((q_ready, k_ready, v_ready)[kind], j)
                    if kind < 2:
                        proj(c0 + e, i, per, 2 * kind, xg, 4, 4 * q, 256, q == 0)
                    else:
                        proj_tokens(c0 + e, i, per, ((psum[:, 4, 0:T], True), (psum[:, 4, T:2 * T], False)), 4, 4 * q, 256, q == 0)
                    if e == 0 and not first:
                        l0_tri(j - 1)
                    if e == 2 and first:
                        stat(0, 7)
                    if e == 2 and not first:
                        l0_av(j - 1)
                    if e == 9:
                        if first:
                            pe.wait_ge(id_ready, 1)
                        l0_logits(j)

            l0_pair(0, None, 0, True)
            with pe.Fori(1, PAIRS) as i:
                l0_pair(i, i, 12, False)

            def l0_tail(e):
                if e == 0:
                    l0_tri(PAIRS - 1)
                if e == 2:
                    l0_av(PAIRS - 1)

            def wo0_ready(e):
                if e == 0:
                    pe.wait_ge(k_ready, PAIRS)
                pe.wait_ge(att_ready, e + 1)
            out_groups(BASE_WO[0], 0, 8, att, 0, wo0_ready, l0_tail)

            def up_body(layer, i, fi, base, m):
                for e in range(16):
                    if e % 8 == 0:
                        pe.wait_ge(acc_free, GROUPS * layer + 3 + 2 * i + e // 8)
                    if m is not None and e < 8 and e % 2 == 0:
                        pe.wait_ge(xg_ready, 4 * m + e // 2 + 1)
                    if m is not None and e == 8:
                        pe.wait_ge(root_ready, m + 1)
                    proj(base + e, fi, 16, 4 * (e // 8), xg, 2, 2 * (e % 8), 512, e % 8 == 0)
                    if m is not None and e == 4:
                        pe.wait_ge(acc_free, GROUPS * layer + 4)
                        stat(m, 4)

            def mlp_layer(layer):
                base = BASE_WO[layer] + WO
                up_body(layer, 0, None, base, 1 + 2 * layer)
                with pe.Fori(1, UPG) as i:
                    up_body(layer, i, i, base, None)
                out_groups(base + UP, layer, FT // 2, hid, 4 + 2 * UPG,
                           lambda e: pe.wait_ge(h_ready, UPG * layer + e // 2 + 1))

            mlp_layer(0)

            pe.wait_ge(acc_free, GROUPS - 1)
            for e in range(8):
                if e % 2 == 0:
                    pe.wait_ge(xg_ready, 8 + e // 2 + 1)
                proj_tokens(BASE_L1 + e, None, 0, ((psum[:, 0, :], True), (psum[:, 1, :], True)), 2, 2 * e, 512, e == 0)
                if e == 4:
                    pe.wait_ge(acc_free, GROUPS)
                    stat(2, 4)
            kbase = BASE_L1 + L1V
            for e in range(2):
                proj(kbase + e, None, 0, 2, xg, 8, 8 * e, P, e == 0)
            pe.wait_ge(wi_lo_s, 1)
            for k in range(KT):
                for th in range(2):
                    o = psum[:, 5, th * NH:(th + 1) * NH]
                    x_hi, x_lo = xg[:, k, th * P:(th + 1) * P], xg[:, k, T + th * P:T + (th + 1) * P]
                    mm(o, x_hi, wi_hi[:, k, :], k == 0 and th == 0)
                    mm(o, x_hi, wi_lo[:, k, :])
                    last = mm(o, x_lo, wi_hi[:, k, :])
            last.then_inc(wi_acc, 1)
            qibase = kbase + L1KI

            def rotate(B, nh, nb, t_av=None):
                pe.wait_ge(rb_u, nb + 1) if nb is not None else pe.wait_ge(rb_sum, B + 1)
                if t_av is not None:
                    pe.wait_ge(att_ready, PAIRS + t_av)
                mm(psum[:, 4, 0:nh * T], rot, tu[:, 0:nh, :], True).then_inc(rot_ready, 1)
                if nb is not None:
                    pe.wait_ge(rb_sq, nb + 1)
                    if isinstance(nb, int) and nb == 0:
                        pe.wait_ge(wis_ready, 1)
                    mm(psum[:, 5, 0:nh * T], avg_h, usq[:, 0:nh, :], True).then_inc(ms_ready, 1)

            def logits(t):
                pe.wait_ge(qr_ready, t + 2)
                if not (isinstance(t, int) and t == 0):
                    pe.wait_ge(rl_ready, t)
                for h in range(2):
                    mm(psum[:, 6 + h, 0:P], qr[:, h, 0:P], ki[:, 0:P], True)
                    last = mm(psum[:, 6 + h, P:384], qr[:, h, P:T], ki[:, :])
                last.then_inc(lg_ready, 1)

            def scores(t, g):
                pe.wait_ge(qr_ready, t + 12)
                if isinstance(t, int) and t == 0:
                    pe.wait_ge(rl_ready, PAIRS)
                    pe.wait_ge(sel_ready, 2)
                else:
                    pe.wait_ge(pt_ready, t)
                for h in range(2):
                    b = 6 + h
                    mm(psum[:, b, 0:P], qr[:, h, 0:P], k_all[:, bass.ds(g, 1), 0:P], True)
                    mm(psum[:, b, P:384], qr[:, h, P:T], k_all[:, bass.ds(g, 1), :])
                    last = mm(psum[:, b, 0:384], idr[:, :], selm[:, :])
                last.then_inc(s_ready, 1)

            def transposes(t):
                pe.wait_ge(pn_ready, t + 1)
                for h in range(2):
                    for o, c in ((0, 0), (1, 1), (2, 2)):
                        last = pe.transpose(psum[:, 6 + h, o * P:(o + 1) * P], pr[:, h, c * P:(c + 1) * P], ident)
                last.then_inc(tr_ready, 1)

            def values(t, n_v):
                pe.wait_ge(pt_ready, t + 1)
                pe.wait_ge(vcur_ready, n_v)
                pe.wait_ge(qr_ready, t + 13) if not (isinstance(t, int) and t == 7) else pe.wait_ge(att_ready, 15)
                o = psum[:, 4, :].rearrange("p (h t) -> p h t", h=2)
                mm(o, v_cur[:, 0, :], prt[:, :, 0:T], True)
                mm(o[:, :, P:T], v_cur[:, 1, :], prt[:, :, T:384]).then_inc(av_ready, 1)

            def block1(B, i, per, par, prev_nh, prev_nb, t_log, t_score, g_score, t_tr, n_v, base, t_read=None):
                if isinstance(B, int) and B <= 2:
                    pe.wait_ge(v1_ready, 1) if B == 1 else pe.wait_ge(rb_sum, 1)
                else:
                    pe.wait_ge(rb_sum, B - 1)
                for e in range(4):
                    proj(base + e, i, per, 2 * par, xg, 4, 4 * e, 256, e == 0)
                    if e == 1:
                        rotate(B - 1, prev_nh, prev_nb, t_read)
                    if e == 2 and t_tr is not None:
                        transposes(t_tr)
                    if e == 3:
                        if t_log is not None:
                            logits(t_log)
                        if t_tr is not None:
                            values(t_tr, n_v)
                        if t_score is not None:
                            scores(t_score, g_score)

            block1(1, None, 0, 0, 1, 0, None, None, None, None, None, qibase)
            block1(2, None, 0, 1, 2, None, 0, None, None, None, None, qibase + 4)
            with pe.Fori(0, 3) as i:
                block1(3 + 2 * i, i, 8, 0, 2, None, 2 * i + 1, None, None, None, None, qibase + 8)
                block1(4 + 2 * i, i, 8, 1, 2, None, 2 * i + 2, None, None, None, None, qibase + 12)
            block1(9, None, 0, 0, 2, None, 7, None, None, None, None, qibase + 32)
            block1(10, None, 0, 1, 2, 1, None, None, None, None, None, qibase + 36)
            block1(11, None, 0, 0, 2, 2, None, None, None, None, None, qibase + 40)
            block1(12, None, 0, 1, 2, 3, None, 0, 0, None, None, qibase + 44)
            with pe.Fori(0, 3) as i:
                block1(13 + 2 * i, i, 8, 0, 2, 4 + 2 * i, None, 2 * i + 1, i, 2 * i, i + 1, qibase + 48, t_read=2 * i)
                block1(14 + 2 * i, i, 8, 1, 2, 5 + 2 * i, None, 2 * i + 2, i + 1, 2 * i + 1, i + 1, qibase + 52, t_read=2 * i + 1)

            def l1_tail(e):
                if e == 1:
                    rotate(18, 2, 10, 6)
                if e == 2:
                    transposes(6)
                if e == 3:
                    values(6, 4)
                    scores(7, 3)
                if e == 6:
                    transposes(7)
                    values(7, 4)

            def wo1_ready(e):
                if e == 0:
                    pe.wait_ge(rb_sum, 19)
                pe.wait_ge(att_ready, PAIRS + e + 1)
            out_groups(BASE_WO[1], 1, 8, att, 0, wo1_ready, l1_tail)
            mlp_layer(1)


def _pieces(w, kts, cols):
    k, n = w.shape
    return w.reshape(k // (P * kts), kts, P, n // cols, cols).transpose(3, 0, 2, 1, 4).reshape(n // cols, k // (P * kts), P, PIECE)


def _constants():
    s = np.arange(P)
    c = np.zeros((P, NC + P), np.float32)
    c[:, C_TRI:C_TRI + P] = -(s[:, None] >= s[None, :]).astype(np.float32)
    c[:, C_ONE:C_ONE + P] = -1.0
    c[:, C_AVG:C_AVG + P] = 1.0 / P
    c[:, C_ROT:C_ROT + P] = (s[:, None] == (s[None, :] + P // 2) % P)
    c[:, C_ID:C_ID + P] = np.eye(P)
    c[:, C_SBM:C_SBM + P] = np.where(s[:, None] >= s[None, :], -BIG, 0.0)
    causal = np.where(s[None, :] > s[:, None], -BIG, 0.0)
    c[:, C_CM:C_CM + P] = causal
    c[:, C_CM + 2 * P:C_CM + 3 * P] = causal
    inv = (1.0 / (np.float32(10000.0) ** (np.arange(0, P, 2, dtype=np.float32) / np.float32(P)))).astype(np.float32)
    ang = (np.arange(T, dtype=np.float32)[:, None] * inv[None, :]).T
    c[:, C_COS:C_COS + T] = np.concatenate([np.cos(ang), np.cos(ang)])
    c[:, C_SIN:C_SIN + T] = np.concatenate([-np.sin(ang), np.sin(ang)])
    c[:, NC:NC + P] = 1.0 / D
    return c


def kernel(x, attn_norm_g, ffn_norm_g, sb_w_qkv, sb_w_o, dsa_w_in, dsa_q_norm_g, dsa_k_norm_g, dsa_ik_norm_g, dsa_w_o,
           ffn_w_up, ffn_conv_w, ffn_conv_b, ffn_w_down):
    import concourse.bacc as bacc
    from concourse.bass_utils import run_bass_kernel_spmd

    a = {k: np.asarray(v) for k, v in dict(
        x=x, ag=attn_norm_g, fg=ffn_norm_g, qkv=sb_w_qkv, wo0=sb_w_o, win=dsa_w_in, qg=dsa_q_norm_g, kg=dsa_k_norm_g,
        ig=dsa_ik_norm_g, wo1=dsa_w_o, up=ffn_w_up, cw=ffn_conv_w, cb=ffn_conv_b, dn=ffn_w_down).items()}

    flat = lambda *p: [q.reshape(-1, P, PIECE) for q in p]
    qkv = [_pieces(a["qkv"][0][:, n * D:(n + 1) * D], 4, 256) for n in range(3)]
    win = a["win"][0]
    kv = KVH * P
    q, k, v, qi, kk, wi = np.split(win, np.cumsum([D, kv, kv, D, P]), axis=1)

    def mlp(layer):
        up = a["up"][layer]
        both = np.concatenate([_pieces(up[:, :FF], 2, 512), _pieces(up[:, FF:], 2, 512)], axis=1)
        return flat(both, _pieces(a["dn"][layer], 2, 512))

    w_all = np.concatenate(
        flat(np.concatenate(qkv, axis=1), _pieces(a["wo0"][0], 2, 512)) + mlp(0)
        + flat(_pieces(v, 2, 512), _pieces(kk, 8, P), _pieces(qi, 4, 256), _pieces(k, 4, 256), _pieces(q, 4, 256),
               _pieces(a["wo1"][0], 2, 512)) + mlp(1))
    assert w_all.shape == (NPIECES, P, PIECE)

    gains = [g.reshape(KT, P).T for g in (a["ag"][0], a["fg"][0], a["ag"][1], a["fg"][1])]
    taps = np.concatenate([a["cw"], a["cb"][:, None]], axis=1)
    taps = taps.reshape(2, 4, 2, UPG, 4, P).transpose(5, 0, 3, 2, 4, 1).reshape(P, -1)
    dsa = [a[n][0] for n in ("qg", "kg", "ig")]
    dsa += [np.roll(g, P // 2) for g in dsa]
    vecs = np.concatenate(gains + [taps, np.stack(dsa, axis=1), np.full((P, 1), EPS, np.float32)], axis=1)
    ins = {
        "x_in": a["x"][0].T.reshape(KT, P, T).transpose(1, 0, 2),
        "w_all": w_all,
        "wi_in": wi.reshape(KT, P, NH).transpose(1, 0, 2),
        "vecs_in": vecs,
        "consts_in": _constants(),
    }
    ins = {n: np.ascontiguousarray(v) for n, v in ins.items()}
    nc = bacc.Bacc("TRN2", target_bir_lowering=False, num_devices=1)
    aps = {n: nc.dram_tensor(n, v.shape, F32, kind="ExternalInput").ap() for n, v in ins.items()}
    out = nc.dram_tensor("out_t", (P, KT, T), F32, kind="ExternalOutput").ap()
    build(nc, **aps, out=out)
    r = run_bass_kernel_spmd(nc, [ins], core_ids=[0])
    o = r.results[0]["out_t"]
    return np.ascontiguousarray(o.transpose(2, 1, 0).reshape(1, T, D))
```

```python
from contextlib import ExitStack

import numpy as np

import concourse.bass as bass
from concourse import mybir

F32 = mybir.dt.float32
F32R = mybir.dt.float32r
ALU = mybir.AluOpType
ACT = mybir.ActivationFunctionType
AX = mybir.AxisListType

P = 128
D = 2048
T = 256
KT = D // P
FF = 5632
FT = FF // P
NH = 16
PAIRS = NH // 2
KVH = 4
TOPK = min(256, T // 4)
EPS = 1e-6
ATT_SCALE = float(P) ** -0.5
WI_SCALE = float(P) ** -0.5 * float(NH) ** -0.5
BIG = 1e30
PIECE = 1024
RING = 4

QKV0 = PAIRS * 12
WO = 4 * 8
UPG = FF // 512
UP = UPG * 16
DN = 4 * (FT // 2)
L1V, L1KI, L1QI, L1K, L1Q = 8, 4, PAIRS * 4, 8, PAIRS * 4
BASE_WO = (QKV0, QKV0 + WO + UP + DN + L1V + L1KI + L1QI + L1K + L1Q)
BASE_L1 = QKV0 + WO + UP + DN
NPIECES = BASE_WO[1] + WO + UP + DN
GROUPS = 4 + 2 * UPG + 4

V_GAIN = 0
V_CONV = 4 * KT
V_DSA = V_CONV + 2 * UPG * 32
NV = V_DSA + 3
C_TRI, C_ONE, C_AVG, C_ID, C_SBM, C_CM, C_COS, C_SIN = 0, 128, 256, 384, 512, 640, 1024, 1280
NC = 1536


def build(nc, x_in, w_all, vecs_in, consts_in, out):
    with ExitStack() as ctx:
        def sb(name, shape, dt=F32, to=ctx):
            return to.enter_context(nc.sbuf_tensor(name, shape, dt))

        def sem(name):
            return ctx.enter_context(nc.semaphore(name))

        psum = ctx.enter_context(nc.psum_tensor("psum", [P, 8, 512], F32))

        raw = sb("raw", [P, RING, PIECE])
        w_hi = sb("w_hi", [P, RING, PIECE], F32R)
        w_lo = sb("w_lo", [P, RING, PIECE], F32R)
        xres = sb("xres", [P, KT, T])
        xg = sb("xg", [P, KT, 2 * T], F32R)
        vecs = sb("vecs", [P, NV + 1])
        avg_d = sb("avg_d", [P, P])
        rs = sb("rs", [P, T + 2])
        part = sb("part", [P, 4, T])
        upad = sb("upad", [P, 4, T + 2])
        conv = sb("conv", [P, 4, T])
        gates = sb("gates", [P, 4, T])

        with ExitStack() as mlp:
            hid = sb("hid", [P, FT, 2 * T], F32R, mlp)
        att_ctx = ctx.enter_context(ExitStack())
        att = sb("att", [P, NH, 2 * T], F32R, att_ctx)
        cst = sb("cst", [P, NC], F32, att_ctx)
        idr = sb("idr", [P, P], F32R, att_ctx)
        with ExitStack() as l0:
            sbm_r = sb("sbm_r", [P, P], F32R, l0)
            rsq = sb("rsq", [P, T], F32, l0)
            tq = sb("tq", [P, 2, T], F32, l0)
            tk = sb("tk", [P, 2, T], F32, l0)
            q0 = sb("q0", [P, 2, T], F32, l0)
            k0 = sb("k0", [P, 2, T], F32, l0)
            v0 = sb("v0", [P, 2, T], F32, l0)
            az = sb("az", [P, 2, 384], F32, l0)
            sp = sb("sp", [P, 2, 384], F32, l0)
            aw = sb("aw", [P, 2, 384], F32, l0)
        l1 = att_ctx
        v_all = sb("v_all", [P, 2, 512], F32, l1)
        v_cur = sb("v_cur", [P, 2, P], F32, l1)
        k_all = sb("k_all", [P, KVH, T], F32, l1)
        ki = sb("ki", [P, T], F32, l1)
        tu = sb("tu", [P, 2, T], F32, l1)
        usq = sb("usq", [P, 2, T], F32, l1)
        rsn = sb("rsn", [P, 2, T], F32, l1)
        ra = sb("ra", [P, 2, T], F32, l1)
        rb = sb("rb", [P, 2, T], F32, l1)
        qr = sb("qr", [P, 2, T], F32, l1)
        rl = sb("rl", [P, 2, 384], F32, l1)
        score = sb("score", [P, 384], F32, l1)
        work = sb("work", [P, 384], F32, l1)
        cum = sb("cum", [P, 384], F32, l1)
        ones = sb("ones", [P, 256], F32, l1)
        top8 = sb("top8", [P, 2, 8], F32, l1)
        tk_n = sb("tk_n", [P, 2, 2], F32, l1)
        selm = sb("selm", [P, 384], F32R, l1)
        pr = sb("pr", [P, 2, 384], F32, l1)
        prt = sb("prt", [P, 2, 384], F32, l1)
        mx = sb("mx", [P, 2, 2], F32, l1)
        nmx = sb("nmx", [P, 2, 2], F32, l1)
        sums = sb("sums", [P, 2, 2], F32, l1)
        rc = sb("rc", [P, 2, 2], F32, l1)
        rope_c = sb("rope_c", [P, 3, T], F32, l1)
        rope_s = sb("rope_s", [P, 3, T], F32, l1)
        wi_t = sb("wi_t", [P, T], F32, l1)
        wi_s = sb("wi_s", [P, 2, NH], F32, l1)
        rcs = sb("rcs", [P, 2], F32, l1)

        raw_full = [sem(f"raw_full{s}") for s in range(RING)]
        hi_ready, lo_ready, piece_used = sem("hi_ready"), sem("lo_ready"), sem("piece_used")
        gains_in, vecs_in_s, avg_in, cst_in = sem("gains_loaded"), sem("vecs_loaded"), sem("avg_loaded"), sem("cst_loaded")
        x_loaded = [sem(f"x_loaded{g}") for g in range(4)]
        stored, pads_zero, ones_set = sem("stored"), sem("pads_zero"), sem("ones_set")
        acc_free, b_copied = sem("acc_free"), sem("b_copied")
        x_ready, sq_ready, sqsum_ready = sem("x_ready"), sem("sq_ready"), sem("sqsum_ready")
        xhi_ready, xg_ready = sem("xhi_ready"), sem("xg_ready")
        stat_ready, root_ready, rs_ready = sem("stat_ready"), sem("root_ready"), sem("rs_ready")
        rsq_ready, id_ready = sem("rsq_ready"), sem("id_ready")
        ub_copied, up_scaled, tap0, tap1, tap2 = sem("ub_copied"), sem("up_scaled"), sem("tap0"), sem("tap1"), sem("tap2")
        silu_ready, gated, h_hi, h_ready = sem("silu_ready"), sem("gated"), sem("h_hi"), sem("h_ready")
        up_sum = sem("up_sum")
        qb_copied, kb_copied, q_sum, k_sum = sem("qb_copied"), sem("kb_copied"), sem("q_sum"), sem("k_sum")
        q_ready, k_ready, v_ready = sem("q_ready"), sem("k_ready"), sem("v_ready")
        z_ready, az_ready, e_ready, l_ready, sp_ready = (sem(n) for n in ("z_ready", "az_ready", "e_ready", "l_ready", "sp_ready"))
        la_ready, a_ready, o_ready = sem("la_ready"), sem("a_ready"), sem("o_ready")
        att_hi, att_ready = sem("att_hi"), sem("att_ready")
        v1_ready, vcur_ready = sem("v1_ready"), sem("vcur_ready")
        tables_ready = sem("tables_ready")
        wi_copied, wi_sum, wi_turned, rcs_s, wis_ready = (sem(n) for n in ("wi_copied", "wi_sum", "wi_turned", "rcs_s", "wis_ready"))
        rb_copied, rb_sum, rb_u, rb_sq = sem("rb_copied"), sem("rb_sum"), sem("rb_u"), sem("rb_sq")
        ms_ready, ln_ready, rsn_ready = sem("ms_ready"), sem("ln_ready"), sem("rsn_ready")
        terms, roped, qr_ready = sem("terms"), sem("roped"), sem("qr_ready")
        lg_ready, rl_ready, sc_half, sc_ready = sem("lg_ready"), sem("rl_ready"), sem("sc_half"), sem("sc_ready")
        topk_s, sel_ready = sem("topk_step"), sem("sel_ready")
        s_ready, mx_ready, nm_ready, p_ready, rc_ready, pn_ready = (sem(n) for n in ("s_ready", "mx_ready", "nm_ready", "p_ready", "rc_ready", "pn_ready"))
        tr_ready, pt_ready, av_ready = sem("tr_ready"), sem("pt_ready"), sem("av_ready")

        wg = w_all.rearrange("n p k -> p n k")
        tri, neg_one = cst[:, C_TRI:C_TRI + P], cst[:, C_ONE:C_ONE + P]
        avg_h, ident = cst[:, C_AVG:C_AVG + P], cst[:, C_ID:C_ID + P]
        cmask = cst[:, C_CM:C_CM + 384]
        cos_t, sin_t = cst[:, C_COS:C_COS + T], cst[:, C_SIN:C_SIN + T]
        at, width = (0, 128), (128, 256)

        def f32(ap):
            return ap.bitcast(F32)

        def gain(m, tile):
            return vecs[:, bass.ds(V_GAIN + m * KT + tile, 1)]

        def times(i, n):
            return 0 if i is None else i * n

        block = ctx.enter_context(nc.Block())

        @block.sync
        def _(sp_q):
            for n in range(RING):
                sp_q.dma_start(raw[:, n, :], wg[:, n, :]).then_inc(raw_full[n], 16)
            loops = (NPIECES - RING) // RING
            with sp_q.Fori(0, loops) as i:
                for s in range(RING):
                    sp_q.wait_ge(lo_ready, i * RING + s + 1)
                    sp_q.dma_start(raw[:, s, :], wg[:, bass.ds(i * RING + RING + s, 1), :]).then_inc(raw_full[s], 16)
            for n in range(RING * (loops + 1), NPIECES):
                sp_q.wait_ge(lo_ready, n - RING + 1)
                sp_q.dma_start(raw[:, n % RING, :], wg[:, n, :]).then_inc(raw_full[n % RING], 16)

        @block.gpsimd
        def _(pool):
            pool.memset(upad[:, :, 0:2], 0.0).then_inc(pads_zero, 1)
            for g in range(4):
                pool.wait_ge(x_ready, 12 + g + 1)
                pool.dma_start(out[:, 4 * g:4 * g + 4, :], xres[:, 4 * g:4 * g + 4, :]).then_inc(stored, 16)
            pool.wait_ge(stored, 64)

        @block.scalar
        def _(act):
            def split(c, i=None, per=0):
                if c >= NPIECES:
                    return
                act.wait_ge(raw_full[c % RING], times(i, 16 * per // RING) + 16 * (c // RING + 1))
                if c >= RING or i is not None:
                    act.wait_ge(piece_used, times(i, per) + c - RING + 1)
                act.copy(w_hi[:, c % RING, :], raw[:, c % RING, :]).then_inc(hi_ready, 1)

            def norm(m, g):
                n = 4 * m + g
                if m == 0:
                    act.wait_ge(x_loaded[g], 16)
                else:
                    act.wait_ge(x_ready, n - 4 + 1)
                for k in range(4):
                    act.activation(xg[:, 4 * g + k, 0:T], xres[:, 4 * g + k, :], ACT.Copy, scale=gain(m, 4 * g + k)).then_inc(xhi_ready, 1)
                if m == 0:
                    split(g)
                if not (m == 0 and g == 0):
                    act.wait_ge(sqsum_ready, n)
                act.activation(conv[:, :, :], xres[:, 4 * g:4 * g + 4, :], ACT.Square).then_inc(sq_ready, 1)

            def root(m, bank):
                act.wait_ge(stat_ready, m + 1)
                act.activation(rs[:, :], psum[:, bank, 0:T + 2], ACT.Sqrt, bias=eps_ap).then_inc(root_ready, 1)

            def copy_b(group, bank0, last_piece):
                act.wait_ge(piece_used, last_piece + 1)
                act.wait_ge(x_ready, group) if group else None
                act.copy(part[:, :, :], psum[:, bank0:bank0 + 4, T:2 * T]).then_inc(b_copied, 1)

            def out_groups(base, per, m, e0=0, tail=None):
                for g in range(4):
                    for e in range(e0 if g == 0 else 0, per):
                        c = base + g * per + e
                        split(c + RING)
                        if tail and g == 0:
                            tail(e)
                        if g and e == 0 and m < 4:
                            norm(m, g - 1)
                    copy_b(4 * (m - 1) + g, 4 * (g % 2), base + g * per + per - 1)

            eps_ap = vecs[:, NV:NV + 1]

            act.dma_start(vecs[:, 0:V_CONV], vecs_in[:, 0:V_CONV]).then_inc(gains_in, 16)
            act.dma_start(xres[:, 0:4, :], x_in[:, 0:4, :]).then_inc(x_loaded[0], 16)
            for g in range(1, 4):
                act.dma_start(xres[:, 4 * g:4 * g + 4, :], x_in[:, 4 * g:4 * g + 4, :]).then_inc(x_loaded[g], 16)
            act.dma_start(avg_d[:, :], consts_in[:, NC:NC + P]).then_inc(avg_in, 16)
            act.dma_start(vecs[:, V_CONV:], vecs_in[:, V_CONV:]).then_inc(vecs_in_s, 16)
            act.dma_start(cst[:, :], consts_in[:, 0:NC]).then_inc(cst_in, 16)
            act.wait_ge(gains_in, 16)
            for g in range(4):
                norm(0, g)

            def l0_ab(j):
                act.wait_ge(la_ready, j + 1)
                if not isinstance(j, int) or j > 0:
                    act.wait_ge(o_ready, j)
                act.activation(aw[:, :, :], psum[:, 5:7, 0:384], ACT.Exp).then_inc(a_ready, 1)

            def l0_out(j):
                act.wait_ge(o_ready, j + 1)
                act.copy(att[:, bass.ds(2 * j, 2), 0:T], psum[:, 7, :].rearrange("p (h t) -> p h t", h=2)).then_inc(att_hi, 1)

            def l0_pair(j, i, per, first):
                for e in range(12):
                    split((0 if i is not None else 0) + e + RING + (0 if i is not None else 12 * j), i, per)
                    n0 = 12 * j
                    if e == 0 and not first:
                        l0_ab(j - 1)
                    if e == 2 and first:
                        root(0, 7)
                        act.preload_act_table_set("natural_log_exp_and_others")
                    if e == 2 and not first:
                        l0_out(j - 1)
                    if e == 3:
                        act.wait_ge(piece_used, n0 + 4)
                        if not first:
                            act.wait_ge(q_ready, j)
                        act.copy(tq[:, :, :], psum[:, 0:2, T:2 * T]).then_inc(qb_copied, 1)
                    if e == 7:
                        act.wait_ge(piece_used, n0 + 8)
                        if not first:
                            act.wait_ge(k_ready, j)
                        act.copy(tk[:, :, :], psum[:, 2:4, T:2 * T]).then_inc(kb_copied, 1)
                    if e == 9:
                        act.wait_ge(z_ready, j + 1)
                        if not first:
                            act.wait_ge(sp_ready, j)
                        act.activation(az[:, :, :], psum[:, 5:7, 0:384], ACT.Abs).then_inc(az_ready, 1)
                        act.wait_ge(az_ready, j + 1)
                        act.activation(az[:, :, :], az[:, :, :], ACT.Exp, scale=-1.0).then_inc(e_ready, 1)
                        act.wait_ge(e_ready, j + 1)
                        act.activation(az[:, :, :], az[:, :, :], ACT.Ln, bias=1.0).then_inc(l_ready, 1)
                    if e == 11:
                        act.wait_ge(piece_used, n0 + 12)
                        if not first:
                            act.wait_ge(o_ready, j)
                        act.wait_ge(rs_ready, 1)
                        for st in range(2):
                            last = act.activation(v0[:, st, :], psum[:, 4, st * T:(st + 1) * T], ACT.Copy, scale=rs[:, T + st:T + st + 1])
                        last.then_inc(v_ready, 1)

            act.wait_ge(cst_in, 16)
            act.copy(idr[:, :], ident)
            act.copy(sbm_r[:, :], cst[:, C_SBM:C_SBM + P]).then_inc(id_ready, 1)
            l0_pair(0, None, 0, True)
            with act.Fori(1, PAIRS) as i:
                l0_pair(i, i, 12, False)

            def l0_tail(e):
                if e == 0:
                    l0_ab(PAIRS - 1)
                if e == 2:
                    l0_out(PAIRS - 1)
            out_groups(BASE_WO[0], 8, 1, 0, l0_tail)

            def conv_scalars(layer, i, val, k, j):
                return vecs[:, bass.ds(V_CONV + layer * UPG * 32 + times(i, 32) + val * 16 + k * 4 + j, 1)]

            def up_slot(layer, i, e, base):
                val = int(e >= 15)
                u = 2 * UPG * layer + 2 * i + val
                f = UPG * layer + i
                if e in (7, 15):
                    act.wait_ge(piece_used, base + 16 * i + e + 1)
                    act.copy(part[:, :, :], psum[:, 4 * val:4 * val + 4, T:2 * T]).then_inc(ub_copied, 1)
                if e in (8, 16):
                    act.wait_ge(up_scaled, u + 1)
                    for k in range(4):
                        last = act.activation(conv[:, k, :], upad[:, k, 0:T], ACT.Identity,
                                              scale=conv_scalars(layer, i, val, k, 0), bias=conv_scalars(layer, i, val, k, 3))
                    last.then_inc(tap0, 1)
                if e == 10:
                    act.wait_ge(tap2, u + 1)
                    act.activation(gates[:, :, :], conv[:, :, :], ACT.Silu).then_inc(silu_ready, 1)
                if e == 19:
                    act.wait_ge(gated, f + 1)
                    act.copy(hid[:, bass.ds(4 * i, 4), 0:T], gates[:, :, :]).then_inc(h_hi, 1)

            def mlp_layer(layer):
                base = BASE_WO[layer] + WO
                m = 1 + 2 * layer
                for e in range(7):
                    split(base + e + RING)
                    if e == 0:
                        norm(m, 3)
                    if e == 4:
                        root(m, 4)
                        act.preload_act_table_set("silu_and_others")
                if layer == 0:
                    act.wait_ge(vecs_in_s, 16)
                with act.Fori(0, UPG) as i:
                    for e in range(7, 23):
                        split(base + e + RING, i, 16)
                        up_slot(layer, i, e, base)
                out_groups(base + UP, FT // 2, 2 + 2 * layer, 7)

            mlp_layer(0)

            act.dma_start(cst[:, :], consts_in[:, 0:NC]).then_inc(cst_in, 16)
            for e in range(8):
                split(BASE_L1 + e + RING)
                if e == 0:
                    norm(2, 3)
                    act.wait_ge(cst_in, 32)
                    act.copy(idr[:, :], ident).then_inc(id_ready, 1)
                if e == 4:
                    root(2, 4)
                    act.preload_act_table_set("natural_log_exp_and_others")
                if e == 7:
                    act.wait_ge(piece_used, BASE_L1 + 8)
                    act.wait_ge(rs_ready, 3)
                    for st in range(2):
                        last = act.activation(v_all[:, st, :], psum[:, st, :], ACT.Copy, scale=rs[:, T + st:T + st + 1])
                    last.then_inc(v1_ready, 1)

            def evac(B, bank0, nh, last_piece, nb):
                act.wait_ge(piece_used, last_piece + 1)
                if not (isinstance(B, int) and B == 0):
                    act.wait_ge(qr_ready, B)
                act.copy(tu[:, 0:nh, :], psum[:, bank0:bank0 + nh, T:2 * T]).then_inc(rb_copied, 1)
                if nb is not None:
                    act.wait_ge(rb_u, nb + 1)
                    act.activation(usq[:, 0:nh, :], tu[:, 0:nh, :], ACT.Square).then_inc(rb_sq, 1)

            def norm_scale(nh, nb):
                act.wait_ge(ms_ready, nb + 1)
                act.activation(rsn[:, 0:nh, :], psum[:, 5, 0:nh * T].rearrange("p (h t) -> p h t", h=nh), ACT.Ln, bias=eps_ap).then_inc(ln_ready, 1)
                act.wait_ge(ln_ready, nb + 1)
                act.activation(rsn[:, 0:nh, :], rsn[:, 0:nh, :], ACT.Exp, scale=-0.5).then_inc(rsn_ready, 1)

            def relu(t):
                act.wait_ge(lg_ready, t + 1)
                act.wait_ge(sc_ready, t + 1)
                act.activation(rl[:, :, :], psum[:, 6:8, 0:384], ACT.Relu).then_inc(rl_ready, 1)

            def exps(t):
                act.wait_ge(nm_ready, t + 1)
                for h in range(2):
                    for th in range(2):
                        c = slice(at[th], at[th] + width[th])
                        last = act.activation(pr[:, h, c], psum[:, 6 + h, c], ACT.Exp, bias=nmx[:, th, h:h + 1], scale=ATT_SCALE,
                                              accum_out=sums[:, th, h:h + 1])
                last.then_inc(p_ready, 1)

            def prt_copy(t):
                act.wait_ge(tr_ready, t + 1)
                act.copy(prt[:, :, :], psum[:, 6:8, 0:384]).then_inc(pt_ready, 1)

            def out_hi(t):
                act.wait_ge(av_ready, t + 1)
                act.copy(att[:, bass.ds(2 * t, 2), 0:T], psum[:, 4, :].rearrange("p (h t) -> p h t", h=2)).then_inc(att_hi, 1)

            def set_v(g):
                act.copy(v_cur[:, :, :], v_all[:, :, bass.ds(g * P, P)]).then_inc(vcur_ready, 1)

            kbase = BASE_L1 + L1V
            for e in range(2):
                split(kbase + e + RING)
            evac(0, 2, 1, kbase + 1, 0)
            for e in range(2, 4):
                split(kbase + e + RING)
            act.wait_ge(piece_used, kbase + 4)
            act.copy(wi_t[:, :], psum[:, 3, T:2 * T]).then_inc(wi_copied, 1)
            qibase = kbase + L1KI

            def block1(B, i, per, par, nb, prev_norm, t_relu, t_soft, t_av, base, v_g=None):
                for e in range(4):
                    split(base + e + RING, i, per)
                    if e == 0 and t_relu is not None:
                        relu(t_relu)
                    if e == 0 and v_g is not None:
                        set_v(v_g)
                    if e == 0 and t_soft is not None:
                        exps(t_soft)
                    if e == 1 and prev_norm is not None:
                        norm_scale(prev_norm[1], prev_norm[0])
                    if e == 2 and t_soft is not None:
                        prt_copy(t_soft)
                    if e == 3:
                        evac(B, 2 * par, 2, base + times(i, per) + 3, nb)
                        if t_av is not None:
                            out_hi(t_av)

            block1(1, None, 0, 0, None, (0, 1), None, None, None, qibase)
            block1(2, None, 0, 1, None, None, None, None, None, qibase + 4)
            with act.Fori(0, 3) as i:
                block1(3 + 2 * i, i, 8, 0, None, None, 2 * i, None, None, qibase + 8)
                block1(4 + 2 * i, i, 8, 1, None, None, 2 * i + 1, None, None, qibase + 12)
            block1(9, None, 0, 0, 1, None, 6, None, None, qibase + 32)
            block1(10, None, 0, 1, 2, (1, 2), 7, None, None, qibase + 36)
            block1(11, None, 0, 0, 3, (2, 2), None, None, None, qibase + 40)
            block1(12, None, 0, 1, 4, (3, 2), None, None, None, qibase + 44)
            with act.Fori(0, 3) as i:
                block1(13 + 2 * i, i, 8, 0, 5 + 2 * i, (4 + 2 * i, 2), None, 2 * i, 2 * i, qibase + 48, v_g=i)
                block1(14 + 2 * i, i, 8, 1, 6 + 2 * i, (5 + 2 * i, 2), None, 2 * i + 1, 2 * i + 1, qibase + 52)

            def l1_tail(e):
                if e == 0:
                    set_v(3)
                    exps(6)
                if e == 1:
                    norm_scale(2, 10)
                if e == 2:
                    prt_copy(6)
                if e == 3:
                    out_hi(6)
                if e == 4:
                    exps(7)
                if e == 6:
                    prt_copy(7)
                    out_hi(7)
            out_groups(BASE_WO[1], 8, 3, 0, l1_tail)
            mlp_layer(1)

        @block.vector
        def _(dve):
            def split(c, i=None, per=0):
                if c >= NPIECES:
                    return
                dve.wait_ge(hi_ready, times(i, per) + c + 1)
                dve.tensor_tensor(w_lo[:, c % RING, :], raw[:, c % RING, :], f32(w_hi[:, c % RING, :]), ALU.subtract).then_inc(lo_ready, 1)

            def norm(m, g):
                n = 4 * m + g
                for k in range(4):
                    dve.wait_ge(xhi_ready, 4 * n + k + 1)
                    last = dve.scalar_tensor_tensor(out=xg[:, 4 * g + k, T:2 * T], in0=xres[:, 4 * g + k, :], scalar=gain(m, 4 * g + k),
                                                    in1=f32(xg[:, 4 * g + k, 0:T]), op0=ALU.mult, op1=ALU.subtract)
                last.then_inc(xg_ready, 1)
                if m == 0:
                    split(g)
                dve.wait_ge(sq_ready, n + 1)
                dve.tensor_reduce(gates[:, g, :], conv[:, :, :].rearrange("p k t -> p t k"), AX.X, ALU.add).then_inc(sqsum_ready, 1)

            def recip(m):
                dve.wait_ge(root_ready, m + 1)
                dve.reciprocal(rs[:, :], rs[:, :]).then_inc(rs_ready, 1)

            def add_group(o, g, bank0):
                dve.wait_ge(b_copied, o + 1)
                dve.tensor_tensor(part[:, :, :], psum[:, bank0:bank0 + 4, 0:T], part[:, :, :], ALU.add).then_inc(acc_free, 1)
                dve.wait_ge(acc_free, GROUPS * (o // 8) + (4 + 2 * UPG) * (o // 4 % 2) + g + 1)
                dve.tensor_tensor(xres[:, 4 * g:4 * g + 4, :], xres[:, 4 * g:4 * g + 4, :], part[:, :, :], ALU.add).then_inc(x_ready, 1)

            def out_groups(base, per, m, e0=0, tail=None):
                for g in range(4):
                    for e in range(e0 if g == 0 else 0, per):
                        split(base + g * per + e + RING)
                        if tail and g == 0:
                            tail(e)
                        if g and e == 1 and m < 4:
                            norm(m, g - 1)
                    add_group(4 * (m - 1) + g, g, 4 * (g % 2))

            dve.wait_ge(gains_in, 16)
            for g in range(4):
                dve.wait_ge(x_loaded[g], 16)
                norm(0, g)

            def l0_out(j):
                dve.wait_ge(att_hi, j + 1)
                dst = att[:, bass.ds(2 * j, 2), :]
                dve.tensor_tensor(dst[:, :, T:2 * T], psum[:, 7, :].rearrange("p (h t) -> p h t", h=2), f32(dst[:, :, 0:T]),
                                  ALU.subtract).then_inc(att_ready, 1)

            def over_heads(ap, n=2):
                return ap.unsqueeze(1).to_broadcast([P, n, T])

            def l0_pair(j, i, per, first):
                n0 = None if i is not None else 12 * j
                for e in range(12):
                    split((0 if i is not None else 12 * j) + e + RING, i, per)
                    if e == 2 and first:
                        recip(0)
                        dve.wait_ge(rs_ready, 1)
                        dve.tensor_scalar(rsq[:, :], rs[:, 0:T], ATT_SCALE, None, ALU.mult).then_inc(rsq_ready, 1)
                        dve.wait_ge(rsq_ready, 1)
                    if e == 2 and not first:
                        l0_out(j - 1)
                    for at_e, b_done, tmp, summed, scale, dst, done, bank in (
                            (3, qb_copied, tq, q_sum, rsq[:, :], q0, q_ready, 0), (7, kb_copied, tk, k_sum, rs[:, 0:T], k0, k_ready, 2)):
                        if e == at_e:
                            dve.wait_ge(b_done, j + 1)
                            dve.tensor_tensor(tmp[:, :, :], psum[:, bank:bank + 2, 0:T], tmp[:, :, :], ALU.add).then_inc(summed, 1)
                            dve.wait_ge(summed, j + 1)
                            if not first:
                                dve.wait_ge(z_ready, j)
                            dve.tensor_tensor(dst[:, :, :], tmp[:, :, :], over_heads(scale), ALU.mult).then_inc(done, 1)
                    if e == 10:
                        dve.wait_ge(l_ready, j + 1)
                        if not first:
                            dve.wait_ge(la_ready, j)
                        dve.scalar_tensor_tensor(out=sp[:, :, :], in0=psum[:, 5:7, 0:384], scalar=0.0, in1=az[:, :, :],
                                                 op0=ALU.max, op1=ALU.add).then_inc(sp_ready, 1)

            l0_pair(0, None, 0, True)
            with dve.Fori(1, PAIRS) as i:
                l0_pair(i, i, 12, False)

            def l0_tail(e):
                if e == 2:
                    l0_out(PAIRS - 1)
            out_groups(BASE_WO[0], 8, 1, 0, l0_tail)

            def conv_scalars(layer, i, val, k, j):
                return vecs[:, bass.ds(V_CONV + layer * UPG * 32 + times(i, 32) + val * 16 + k * 4 + j, 1)]

            def up_slot(layer, i, e):
                val = int(e >= 15)
                u = 2 * UPG * layer + 2 * i + val
                f = UPG * layer + i
                if e in (7, 15):
                    dve.wait_ge(ub_copied, u + 1)
                    dve.tensor_tensor(part[:, :, :], psum[:, 4 * val:4 * val + 4, 0:T], part[:, :, :], ALU.add).then_inc(acc_free, 1)
                    dve.wait_ge(acc_free, GROUPS * layer + 4 + 2 * i + val + 1)
                    dve.tensor_tensor(upad[:, :, 2:T + 2], part[:, :, :], over_heads(rs[:, 0:T], 4), ALU.mult).then_inc(up_scaled, 1)
                if e in (9, 17):
                    dve.wait_ge(tap0, u + 1)
                    for j, done in ((1, tap1), (2, tap2)):
                        for k in range(4):
                            last = dve.scalar_tensor_tensor(out=conv[:, k, :], in0=upad[:, k, j:j + T], scalar=conv_scalars(layer, i, val, k, j),
                                                            in1=conv[:, k, :], op0=ALU.mult, op1=ALU.add)
                        last.then_inc(done, 1)
                        dve.wait_ge(done, u + 1)
                if e == 18:
                    dve.wait_ge(silu_ready, f + 1)
                    dve.tensor_tensor(gates[:, :, :], gates[:, :, :], conv[:, :, :], ALU.mult).then_inc(gated, 1)
                if e == 20:
                    dve.wait_ge(h_hi, f + 1)
                    dst = hid[:, bass.ds(4 * i, 4), :]
                    dve.tensor_tensor(dst[:, :, T:2 * T], gates[:, :, :], f32(dst[:, :, 0:T]), ALU.subtract).then_inc(h_ready, 1)

            def mlp_layer(layer):
                base = BASE_WO[layer] + WO
                m = 1 + 2 * layer
                if layer == 0:
                    dve.wait_ge(pads_zero, 1)
                    dve.wait_ge(vecs_in_s, 16)
                for e in range(7):
                    split(base + e + RING)
                    if e == 1:
                        norm(m, 3)
                    if e == 4:
                        recip(m)
                        dve.wait_ge(rs_ready, m + 1)
                with dve.Fori(0, UPG) as i:
                    for e in range(7, 23):
                        split(base + e + RING, i, 16)
                        up_slot(layer, i, e)
                out_groups(base + UP, FT // 2, 2 + 2 * layer, 7)

            mlp_layer(0)

            for e in range(8):
                split(BASE_L1 + e + RING)
                if e == 1:
                    norm(2, 3)
                if e == 2:
                    dve.wait_ge(cst_in, 32)
                    for n in range(3):
                        dve.tensor_scalar(rope_c[:, n, :], cos_t, vecs[:, V_DSA + n:V_DSA + n + 1], None, ALU.mult)
                        last = dve.tensor_scalar(rope_s[:, n, :], sin_t, vecs[:, V_DSA + n:V_DSA + n + 1], None, ALU.mult)
                    last.then_inc(tables_ready, 1)
                    dve.memset(score[:, :], 0.0).then_inc(sc_ready, 1)
                    dve.memset(ones[:, :], 1.0).then_inc(ones_set, 1)
                    dve.wait_ge(ones_set, 1)
                    dve.wait_ge(tables_ready, 1)
                if e == 4:
                    recip(2)
                    dve.wait_ge(rs_ready, 3)
                    dve.tensor_scalar(rcs[:, :], rs[:, T:T + 2], WI_SCALE, None, ALU.mult).then_inc(rcs_s, 1)

            def evac(B, bank0, nh, nb):
                dve.wait_ge(rb_copied, B + 1)
                dve.tensor_tensor(tu[:, 0:nh, :], psum[:, bank0:bank0 + nh, 0:T], tu[:, 0:nh, :], ALU.add).then_inc(rb_sum, 1)
                if nb is not None:
                    dve.wait_ge(rb_sum, B + 1)
                    dve.tensor_tensor(tu[:, 0:nh, :], tu[:, 0:nh, :], over_heads(rs[:, 0:T], nh), ALU.mult).then_inc(rb_u, 1)

            def rope(B, nh, nb, c_t, s_t, dst, after=None):
                if nb is None:
                    dve.wait_ge(rb_sum, B + 1)
                else:
                    dve.wait_ge(rb_u, nb + 1)
                dve.tensor_tensor(ra[:, 0:nh, :], tu[:, 0:nh, :], over_heads(c_t, nh), ALU.mult)
                for lo, hi in ((0, P // 2), (P // 2, 0)):
                    last = dve.tensor_tensor(rb[hi:hi + P // 2, 0:nh, :], tu[lo:lo + P // 2, 0:nh, :],
                                             s_t[lo:lo + P // 2, :].unsqueeze(1).to_broadcast([P // 2, nh, T]), ALU.mult)
                last.then_inc(terms, 1)
                dve.wait_ge(terms, B + 1)
                if after is not None:
                    dve.wait_ge(*after)
                if nb is None:
                    dve.tensor_tensor(dst, ra[:, 0:nh, :], rb[:, 0:nh, :], ALU.add).then_inc(qr_ready, 1)
                else:
                    dve.tensor_tensor(ra[:, 0:nh, :], ra[:, 0:nh, :], rb[:, 0:nh, :], ALU.add).then_inc(roped, 1)
                    dve.wait_ge(roped, nb + 1)
                    dve.wait_ge(rsn_ready, nb + 1)
                    dve.tensor_tensor(dst, ra[:, 0:nh, :], rsn[:, 0:nh, :], ALU.mult).then_inc(qr_ready, 1)

            def rope_prev(B, kind, nb=None):
                if kind == "ki":
                    rope(B, 1, nb, rope_c[:, 2, :], rope_s[:, 2, :], ki[:, :].unsqueeze(1))
                elif kind == "qi":
                    first = isinstance(B, int) and B == 1
                    rope(B, 2, None, cos_t, sin_t, qr[:, :, :], None if first else (lg_ready, B - 1))
                elif kind == "k":
                    rope(B, 2, nb, rope_c[:, 1, :], rope_s[:, 1, :], k_all[:, 2 * (B - 9):2 * (B - 9) + 2, :])
                else:
                    after = (lg_ready, 8) if isinstance(B, int) and B == 11 else (s_ready, B - 11)
                    rope(B, 2, nb, rope_c[:, 0, :], rope_s[:, 0, :], qr[:, :, :], after)

            def add_scores(t):
                dve.wait_ge(rl_ready, t + 1)
                if isinstance(t, int) and t == 0:
                    dve.wait_ge(wis_ready, 1)
                for h in range(2):
                    dve.wait_ge(sc_half if h else sc_ready, t + 1)
                    for th in range(2):
                        c = slice(at[th], at[th] + width[th])
                        last = dve.scalar_tensor_tensor(out=score[:, c], in0=rl[:, h, c], scalar=wi_s[:, th, bass.ds(2 * t + h, 1)],
                                                        in1=score[:, c], op0=ALU.mult, op1=ALU.add)
                    last.then_inc(sc_ready if h else sc_half, 1)

            step = [0]

            def link(ins):
                step[0] += 1
                ins.then_inc(topk_s, 1)
                dve.wait_ge(topk_s, step[0])

            def mask_scores():
                dve.wait_ge(sc_ready, PAIRS + 1)
                link(dve.tensor_tensor(score[:, :], score[:, :], cmask, ALU.add))
                link(dve.tensor_copy(work[:, :], score[:, :]))

            def top_rounds(th, lo, hi):
                w = work[:, at[th]:at[th] + width[th]]
                for r in range(lo, hi):
                    link(dve.max(top8[:, th, :], w))
                    if r < TOPK // 8 - 1:
                        link(dve.match_replace(w, top8[:, th, :], w, -3e38))

            def select(th):
                c = slice(at[th], at[th] + width[th])
                thr = top8[:, th, 7:8]
                link(dve.tensor_scalar(work[:, c], score[:, c], thr, None, ALU.is_gt))
                link(dve.tensor_reduce(tk_n[:, th, 0:1], work[:, c], AX.X, ALU.add))
                link(dve.tensor_scalar(tk_n[:, th, 1:2], tk_n[:, th, 0:1], -1.0, float(TOPK), ALU.mult, ALU.add))
                link(dve.tensor_scalar(score[:, c], score[:, c], thr, None, ALU.is_equal))
                link(dve.tensor_tensor_scan(cum[:, c], ones[:, 0:width[th]], score[:, c], 0.0, ALU.mult, ALU.add))
                link(dve.scalar_tensor_tensor(out=score[:, c], in0=cum[:, c], scalar=tk_n[:, th, 1:2], in1=score[:, c],
                                              op0=ALU.is_le, op1=ALU.mult))
                link(dve.tensor_tensor(work[:, c], work[:, c], score[:, c], ALU.add))
                link(dve.tensor_scalar(work[:, c], work[:, c], -1.0, BIG, ALU.add, ALU.mult))
                dve.tensor_tensor(selm[:, c], work[:, c], cmask[:, c], ALU.add).then_inc(sel_ready, 1)

            def maxes(t):
                dve.wait_ge(s_ready, t + 1)
                for th in range(2):
                    last = dve.tensor_reduce(mx[:, th, :], psum[:, 6:8, at[th]:at[th] + width[th]], AX.X, ALU.max)
                last.then_inc(mx_ready, 1)
                dve.wait_ge(mx_ready, t + 1)
                dve.tensor_scalar(nmx[:, :, :], mx[:, :, :], -ATT_SCALE, None, ALU.mult).then_inc(nm_ready, 1)

            def normalise(t):
                dve.wait_ge(p_ready, t + 1)
                dve.reciprocal(rc[:, :, :], sums[:, :, :]).then_inc(rc_ready, 1)
                dve.wait_ge(rc_ready, t + 1)
                for h in range(2):
                    for th in range(2):
                        c = slice(at[th], at[th] + width[th])
                        last = dve.tensor_scalar(pr[:, h, c], pr[:, h, c], rc[:, th, h:h + 1], None, ALU.mult)
                last.then_inc(pn_ready, 1)

            def out_lo(t):
                dve.wait_ge(att_hi, PAIRS + t + 1)
                dst = att[:, bass.ds(2 * t, 2), :]
                dve.tensor_tensor(dst[:, :, T:2 * T], psum[:, 4, :].rearrange("p (h t) -> p h t", h=2), f32(dst[:, :, 0:T]),
                                  ALU.subtract).then_inc(att_ready, 1)

            kbase = BASE_L1 + L1V
            for e in range(2):
                split(kbase + e + RING)
            evac(0, 2, 1, 0)
            for e in range(2, 4):
                split(kbase + e + RING)
            dve.wait_ge(wi_copied, 1)
            dve.tensor_tensor(wi_t[:, :], psum[:, 3, 0:T], wi_t[:, :], ALU.add).then_inc(wi_sum, 1)

            def index_weights():
                dve.wait_ge(wi_turned, 1)
                dve.wait_ge(rcs_s, 1)
                for th in range(2):
                    last = dve.tensor_scalar(wi_s[:, th, :], psum[:, 4, th * P:th * P + NH], rs[:, T + th:T + th + 1], rcs[:, th:th + 1],
                                             ALU.mult, ALU.mult)
                last.then_inc(wis_ready, 1)
            qibase = kbase + L1KI

            def block1(B, i, per, par, nb, prev, t_score, t_soft, t_av, base, extra=None):
                for e in range(4):
                    split(base + e + RING, i, per)
                    if e == 0 and t_score is not None:
                        add_scores(t_score)
                    if e == 0 and t_soft is not None:
                        maxes(t_soft)
                    if e == 1 and t_soft is not None:
                        normalise(t_soft)
                    if e == 1:
                        rope_prev(B - 1, *prev)
                    if e == 3:
                        evac(B, 2 * par, 2, nb)
                        if t_av is not None:
                            out_lo(t_av)
                    if extra is not None:
                        extra(e)

            def topk_a(e):
                if e == 0:
                    mask_scores()
                if e == 2:
                    top_rounds(1, 0, 4)

            def topk_b(e):
                if e == 0:
                    top_rounds(1, 4, 8)
                if e == 2:
                    top_rounds(0, 0, 8)

            def topk_c(e):
                if e == 0:
                    select(0)
                if e == 2:
                    select(1)

            block1(1, None, 0, 0, None, ("ki", 0), None, None, None, qibase, lambda e: index_weights() if e == 2 else None)
            block1(2, None, 0, 1, None, ("qi",), None, None, None, qibase + 4)
            with dve.Fori(0, 3) as i:
                block1(3 + 2 * i, i, 8, 0, None, ("qi",), 2 * i, None, None, qibase + 8)
                block1(4 + 2 * i, i, 8, 1, None, ("qi",), 2 * i + 1, None, None, qibase + 12)
            block1(9, None, 0, 0, 1, ("qi",), 6, None, None, qibase + 32)
            block1(10, None, 0, 1, 2, ("k", 1), 7, None, None, qibase + 36, topk_a)
            block1(11, None, 0, 0, 3, ("k", 2), None, None, None, qibase + 40, topk_b)
            block1(12, None, 0, 1, 4, ("q", 3), None, None, None, qibase + 44, topk_c)
            with dve.Fori(0, 3) as i:
                block1(13 + 2 * i, i, 8, 0, 5 + 2 * i, ("q", 4 + 2 * i), None, 2 * i, 2 * i, qibase + 48)
                block1(14 + 2 * i, i, 8, 1, 6 + 2 * i, ("q", 5 + 2 * i), None, 2 * i + 1, 2 * i + 1, qibase + 52)

            def l1_tail(e):
                if e == 0:
                    maxes(6)
                if e == 1:
                    normalise(6)
                    rope_prev(18, "q", 10)
                if e == 3:
                    out_lo(6)
                if e == 4:
                    maxes(7)
                if e == 5:
                    normalise(7)
                if e == 6:
                    out_lo(7)
            out_groups(BASE_WO[1], 8, 3, 0, l1_tail)
            mlp_layer(1)

        @block.tensor
        def _(pe):
            def mm(o, lhsT, rhs, start=False):
                return pe.matmul(o, lhsT, rhs, start=start, stop=True, skip_group_check=True)

            def proj(c, i, per, bank0, act_in, kts, k0_, cols, first):
                pe.wait_ge(lo_ready, times(i, per) + c + 1)
                s = c % RING
                for ct in range(cols // P):
                    for kk in range(kts):
                        w = slice(kk * cols + ct * P, kk * cols + (ct + 1) * P)
                        k = k0_ + kk
                        mm(psum[:, bank0 + ct, :], w_hi[:, s, w], act_in[:, k, :], first and kk == 0)
                        last = mm(psum[:, bank0 + ct, 0:T], w_lo[:, s, w], act_in[:, k, 0:T])
                last.then_inc(piece_used, 1)

            def proj_tokens(c, i, per, places, kts, k0_, cols, first):
                pe.wait_ge(lo_ready, times(i, per) + c + 1)
                s = c % RING
                for kk in range(kts):
                    w = slice(kk * cols, (kk + 1) * cols)
                    for th in range(2):
                        k = k0_ + kk
                        new = first and kk == 0 and places[th][1]
                        x_hi, x_lo = xg[:, k, th * P:(th + 1) * P], xg[:, k, T + th * P:T + (th + 1) * P]
                        mm(places[th][0], x_hi, w_hi[:, s, w], new)
                        mm(places[th][0], x_hi, w_lo[:, s, w])
                        last = mm(places[th][0], x_lo, w_hi[:, s, w])
                last.then_inc(piece_used, 1)

            def stat(m, bank):
                pe.wait_ge(sqsum_ready, 4 * (m + 1))
                if m == 0:
                    pe.wait_ge(avg_in, 16)
                for g in range(4):
                    mm(psum[:, bank, 0:T], avg_d[:, :], gates[:, g, :], g == 0)
                for th in range(2):
                    for g in range(4):
                        last = mm(psum[:, bank, T + th:T + th + 1], gates[:, g, th * P:(th + 1) * P], avg_d[:, 0:1])
                last.then_inc(stat_ready, 1)

            def out_groups(base, layer, per, src, n0, ready, tail=None):
                for g in range(4):
                    n = GROUPS * layer + n0 + g
                    if g >= 2 or n0:
                        pe.wait_ge(acc_free, n - 1)
                    for e in range(per):
                        if g == 0:
                            ready(e)
                        proj(base + g * per + e, None, 0, 4 * (g % 2), src, 2, 2 * e, 512, e == 0)
                        if tail and g == 0:
                            tail(e)

            def l0_logits(j):
                pe.wait_ge(q_ready, j + 1)
                pe.wait_ge(k_ready, j + 1)
                if not (isinstance(j, int) and j == 0):
                    pe.wait_ge(a_ready, j)
                for h in range(2):
                    b = 5 + h
                    mm(psum[:, b, 0:T], k0[:, h, 0:P], q0[:, h, :], True)
                    mm(psum[:, b, T:384], k0[:, h, P:T], q0[:, h, P:T])
                    mm(psum[:, b, 0:P], idr[:, :], sbm_r[:, :])
                    last = mm(psum[:, b, T:384], idr[:, :], sbm_r[:, :])
                last.then_inc(z_ready, 1)

            def l0_tri(j):
                pe.wait_ge(sp_ready, j + 1)
                for h in range(2):
                    b = 5 + h
                    mm(psum[:, b, 0:T], tri, sp[:, h, 0:T])
                    mm(psum[:, b, P:T], neg_one, sp[:, h, T:384])
                    last = mm(psum[:, b, T:384], tri, sp[:, h, T:384])
                last.then_inc(la_ready, 1)

            def l0_av(j):
                pe.wait_ge(a_ready, j + 1)
                pe.wait_ge(v_ready, j + 1)
                if not (isinstance(j, int) and j == 0):
                    pe.wait_ge(att_ready, j)
                for h in range(2):
                    mm(psum[:, 7, h * T:(h + 1) * T], v0[:, 0, h * P:(h + 1) * P], aw[:, h, 0:T], h == 0)
                    last = mm(psum[:, 7, h * T + P:(h + 1) * T], v0[:, 1, h * P:(h + 1) * P], aw[:, h, T:384])
                last.then_inc(o_ready, 1)

            def l0_pair(j, i, per, first):
                c0 = 0 if i is not None else 12 * j
                for e in range(12):
                    kind, q = e // 4, e % 4
                    if first and kind == 0:
                        pe.wait_ge(xg_ready, q + 1)
                    if q == 0 and not first:
                        pe.wait_ge((q_ready, k_ready, v_ready)[kind], j)
                    if kind < 2:
                        proj(c0 + e, i, per, 2 * kind, xg, 4, 4 * q, 256, q == 0)
                    else:
                        proj_tokens(c0 + e, i, per, ((psum[:, 4, 0:T], True), (psum[:, 4, T:2 * T], False)), 4, 4 * q, 256, q == 0)
                    if e == 0 and not first:
                        l0_tri(j - 1)
                    if e == 2 and first:
                        stat(0, 7)
                    if e == 2 and not first:
                        l0_av(j - 1)
                    if e == 9:
                        if first:
                            pe.wait_ge(id_ready, 1)
                        l0_logits(j)

            l0_pair(0, None, 0, True)
            with pe.Fori(1, PAIRS) as i:
                l0_pair(i, i, 12, False)

            def l0_tail(e):
                if e == 0:
                    l0_tri(PAIRS - 1)
                if e == 2:
                    l0_av(PAIRS - 1)

            def wo0_ready(e):
                if e == 0:
                    pe.wait_ge(k_ready, PAIRS)
                pe.wait_ge(att_ready, e + 1)
            out_groups(BASE_WO[0], 0, 8, att, 0, wo0_ready, l0_tail)

            def up_body(layer, i, fi, base, m):
                for e in range(16):
                    if e % 8 == 0:
                        pe.wait_ge(acc_free, GROUPS * layer + 3 + 2 * i + e // 8)
                    if m is not None and e < 8 and e % 2 == 0:
                        pe.wait_ge(xg_ready, 4 * m + e // 2 + 1)
                    if m is not None and e == 8:
                        pe.wait_ge(root_ready, m + 1)
                    proj(base + e, fi, 16, 4 * (e // 8), xg, 2, 2 * (e % 8), 512, e % 8 == 0)
                    if m is not None and e == 4:
                        pe.wait_ge(acc_free, GROUPS * layer + 4)
                        stat(m, 4)

            def mlp_layer(layer):
                base = BASE_WO[layer] + WO
                up_body(layer, 0, None, base, 1 + 2 * layer)
                with pe.Fori(1, UPG) as i:
                    up_body(layer, i, i, base, None)
                out_groups(base + UP, layer, FT // 2, hid, 4 + 2 * UPG,
                           lambda e: pe.wait_ge(h_ready, UPG * layer + e // 2 + 1))

            mlp_layer(0)

            pe.wait_ge(acc_free, GROUPS - 1)
            for e in range(8):
                if e % 2 == 0:
                    pe.wait_ge(xg_ready, 8 + e // 2 + 1)
                proj_tokens(BASE_L1 + e, None, 0, ((psum[:, 0, :], True), (psum[:, 1, :], True)), 2, 2 * e, 512, e == 0)
                if e == 4:
                    pe.wait_ge(acc_free, GROUPS)
                    stat(2, 4)
            kbase = BASE_L1 + L1V
            for e in range(2):
                proj(kbase + e, None, 0, 2, xg, 8, 8 * e, P, e == 0)
            for e in range(2):
                proj(kbase + 2 + e, None, 0, 3, xg, 8, 8 * e, P, e == 0)
            qibase = kbase + L1KI

            def mean_squares(nh, nb):
                pe.wait_ge(rb_sq, nb + 1)
                if not (isinstance(nb, int) and nb == 0):
                    pe.wait_ge(rsn_ready, nb)
                mm(psum[:, 5, 0:nh * T], avg_h, usq[:, 0:nh, :], True).then_inc(ms_ready, 1)

            def turn_wi():
                pe.wait_ge(wi_sum, 1)
                for th in range(2):
                    last = pe.transpose(psum[:, 4, th * P:(th + 1) * P], wi_t[:, th * P:(th + 1) * P], ident)
                last.then_inc(wi_turned, 1)

            def logits(t):
                pe.wait_ge(qr_ready, t + 2)
                if not (isinstance(t, int) and t == 0):
                    pe.wait_ge(rl_ready, t)
                for h in range(2):
                    mm(psum[:, 6 + h, 0:P], qr[:, h, 0:P], ki[:, 0:P], True)
                    last = mm(psum[:, 6 + h, P:384], qr[:, h, P:T], ki[:, :])
                last.then_inc(lg_ready, 1)

            def scores(t, g):
                pe.wait_ge(qr_ready, t + 12)
                if isinstance(t, int) and t == 0:
                    pe.wait_ge(rl_ready, PAIRS)
                    pe.wait_ge(sel_ready, 2)
                else:
                    pe.wait_ge(pt_ready, t)
                for h in range(2):
                    b = 6 + h
                    mm(psum[:, b, 0:P], qr[:, h, 0:P], k_all[:, bass.ds(g, 1), 0:P], True)
                    mm(psum[:, b, P:384], qr[:, h, P:T], k_all[:, bass.ds(g, 1), :])
                    last = mm(psum[:, b, 0:384], idr[:, :], selm[:, :])
                last.then_inc(s_ready, 1)

            def transposes(t):
                pe.wait_ge(pn_ready, t + 1)
                for h in range(2):
                    for o, c in ((0, 0), (1, 1), (2, 2)):
                        last = pe.transpose(psum[:, 6 + h, o * P:(o + 1) * P], pr[:, h, c * P:(c + 1) * P], ident)
                last.then_inc(tr_ready, 1)

            def values(t, n_v):
                pe.wait_ge(pt_ready, t + 1)
                pe.wait_ge(vcur_ready, n_v)
                pe.wait_ge(att_ready, PAIRS + t)
                o = psum[:, 4, :].rearrange("p (h t) -> p h t", h=2)
                mm(o, v_cur[:, 0, :], prt[:, :, 0:T], True)
                mm(o[:, :, P:T], v_cur[:, 1, :], prt[:, :, T:384]).then_inc(av_ready, 1)

            def block1(B, i, per, par, prev_nh, prev_nb, t_log, t_score, g_score, t_tr, n_v, base):
                if isinstance(B, int) and B == 1:
                    pe.wait_ge(v1_ready, 1)
                elif isinstance(B, int) and B == 2:
                    pe.wait_ge(wi_sum, 1)
                else:
                    pe.wait_ge(rb_sum, B - 1)
                for e in range(4):
                    proj(base + e, i, per, 2 * par, xg, 4, 4 * e, 256, e == 0)
                    if e == 1 and prev_nb is not None:
                        mean_squares(prev_nh, prev_nb)
                    if e == 1 and isinstance(B, int) and B == 1:
                        turn_wi()
                    if e == 2 and t_tr is not None:
                        transposes(t_tr)
                    if e == 3:
                        if t_log is not None:
                            logits(t_log)
                        if t_tr is not None:
                            values(t_tr, n_v)
                        if t_score is not None:
                            scores(t_score, g_score)

            block1(1, None, 0, 0, 1, 0, None, None, None, None, None, qibase)
            block1(2, None, 0, 1, 2, None, 0, None, None, None, None, qibase + 4)
            with pe.Fori(0, 3) as i:
                block1(3 + 2 * i, i, 8, 0, 2, None, 2 * i + 1, None, None, None, None, qibase + 8)
                block1(4 + 2 * i, i, 8, 1, 2, None, 2 * i + 2, None, None, None, None, qibase + 12)
            block1(9, None, 0, 0, 2, None, 7, None, None, None, None, qibase + 32)
            block1(10, None, 0, 1, 2, 1, None, None, None, None, None, qibase + 36)
            block1(11, None, 0, 0, 2, 2, None, None, None, None, None, qibase + 40)
            block1(12, None, 0, 1, 2, 3, None, 0, 0, None, None, qibase + 44)
            with pe.Fori(0, 3) as i:
                block1(13 + 2 * i, i, 8, 0, 2, 4 + 2 * i, None, 2 * i + 1, i, 2 * i, i + 1, qibase + 48)
                block1(14 + 2 * i, i, 8, 1, 2, 5 + 2 * i, None, 2 * i + 2, i + 1, 2 * i + 1, i + 1, qibase + 52)

            def l1_tail(e):
                if e == 1:
                    mean_squares(2, 10)
                if e == 2:
                    transposes(6)
                if e == 3:
                    values(6, 4)
                    scores(7, 3)
                if e == 6:
                    transposes(7)
                    values(7, 4)

            def wo1_ready(e):
                if e == 0:
                    pe.wait_ge(rb_sum, 19)
                pe.wait_ge(att_ready, PAIRS + e + 1)
            out_groups(BASE_WO[1], 1, 8, att, 0, wo1_ready, l1_tail)
            mlp_layer(1)


def _pieces(w, kts, cols):
    k, n = w.shape
    return w.reshape(k // (P * kts), kts, P, n // cols, cols).transpose(3, 0, 2, 1, 4).reshape(n // cols, k // (P * kts), P, PIECE)


def _constants():
    s = np.arange(P)
    c = np.zeros((P, NC + P), np.float32)
    c[:, C_TRI:C_TRI + P] = -(s[:, None] >= s[None, :]).astype(np.float32)
    c[:, C_ONE:C_ONE + P] = -1.0
    c[:, C_AVG:C_AVG + P] = 1.0 / P
    c[:, C_ID:C_ID + P] = np.eye(P)
    c[:, C_SBM:C_SBM + P] = np.where(s[:, None] >= s[None, :], -BIG, 0.0)
    causal = np.where(s[None, :] > s[:, None], -BIG, 0.0)
    c[:, C_CM:C_CM + P] = causal
    c[:, C_CM + 2 * P:C_CM + 3 * P] = causal
    inv = (1.0 / (np.float32(10000.0) ** (np.arange(0, P, 2, dtype=np.float32) / np.float32(P)))).astype(np.float32)
    ang = (np.arange(T, dtype=np.float32)[:, None] * inv[None, :]).T
    c[:, C_COS:C_COS + T] = np.concatenate([np.cos(ang), np.cos(ang)])
    c[:, C_SIN:C_SIN + T] = np.concatenate([np.sin(ang), -np.sin(ang)])
    c[:, NC:NC + P] = 1.0 / D
    return c


def kernel(x, attn_norm_g, ffn_norm_g, sb_w_qkv, sb_w_o, dsa_w_in, dsa_q_norm_g, dsa_k_norm_g, dsa_ik_norm_g, dsa_w_o,
           ffn_w_up, ffn_conv_w, ffn_conv_b, ffn_w_down):
    import concourse.bacc as bacc
    from concourse.bass_utils import run_bass_kernel_spmd

    a = {k: np.asarray(v) for k, v in dict(
        x=x, ag=attn_norm_g, fg=ffn_norm_g, qkv=sb_w_qkv, wo0=sb_w_o, win=dsa_w_in, qg=dsa_q_norm_g, kg=dsa_k_norm_g,
        ig=dsa_ik_norm_g, wo1=dsa_w_o, up=ffn_w_up, cw=ffn_conv_w, cb=ffn_conv_b, dn=ffn_w_down).items()}

    flat = lambda *p: [q.reshape(-1, P, PIECE) for q in p]
    qkv = [_pieces(a["qkv"][0][:, n * D:(n + 1) * D], 4, 256) for n in range(3)]
    win = a["win"][0]
    kv = KVH * P
    q, k, v, qi, kk, wi = np.split(win, np.cumsum([D, kv, kv, D, P]), axis=1)

    def mlp(layer):
        up = a["up"][layer]
        both = np.concatenate([_pieces(up[:, :FF], 2, 512), _pieces(up[:, FF:], 2, 512)], axis=1)
        return flat(both, _pieces(a["dn"][layer], 2, 512))

    w_all = np.concatenate(
        flat(np.concatenate(qkv, axis=1), _pieces(a["wo0"][0], 2, 512)) + mlp(0)
        + flat(_pieces(v, 2, 512), _pieces(kk, 8, P), _pieces(np.pad(wi, ((0, 0), (0, P - NH))), 8, P), _pieces(qi, 4, 256), _pieces(k, 4, 256), _pieces(q, 4, 256),
               _pieces(a["wo1"][0], 2, 512)) + mlp(1))
    assert w_all.shape == (NPIECES, P, PIECE)

    gains = [g.reshape(KT, P).T for g in (a["ag"][0], a["fg"][0], a["ag"][1], a["fg"][1])]
    taps = np.concatenate([a["cw"], a["cb"][:, None]], axis=1)
    taps = taps.reshape(2, 4, 2, UPG, 4, P).transpose(5, 0, 3, 2, 4, 1).reshape(P, -1)
    dsa = [a[n][0] for n in ("qg", "kg", "ig")]
    vecs = np.concatenate(gains + [taps, np.stack(dsa, axis=1), np.full((P, 1), EPS, np.float32)], axis=1)
    ins = {
        "x_in": a["x"][0].T.reshape(KT, P, T).transpose(1, 0, 2),
        "w_all": w_all,
        "vecs_in": vecs,
        "consts_in": _constants(),
    }
    ins = {n: np.ascontiguousarray(v) for n, v in ins.items()}
    nc = bacc.Bacc("TRN2", target_bir_lowering=False, num_devices=1)
    aps = {n: nc.dram_tensor(n, v.shape, F32, kind="ExternalInput").ap() for n, v in ins.items()}
    out = nc.dram_tensor("out_t", (P, KT, T), F32, kind="ExternalOutput").ap()
    build(nc, **aps, out=out)
    r = run_bass_kernel_spmd(nc, [ins], core_ids=[0])
    o = r.results[0]["out_t"]
    return np.ascontiguousarray(o.transpose(2, 1, 0).reshape(1, T, D))
```

```python
from contextlib import ExitStack

import numpy as np

import concourse.bass as bass
from concourse import mybir

F32 = mybir.dt.float32
F32R = mybir.dt.float32r
ALU = mybir.AluOpType
ACT = mybir.ActivationFunctionType
AX = mybir.AxisListType

P = 128
D = 2048
T = 256
KT = D // P
FF = 5632
FT = FF // P
NH = 16
PAIRS = NH // 2
KVH = 4
TOPK = min(256, T // 4)
TOPK_STEPS = 2 * (2 + 2 * (TOPK // 8) - 1 + 8)
EPS = 1e-6
ATT_SCALE = float(P) ** -0.5
WI_SCALE = float(P) ** -0.5 * float(NH) ** -0.5
BIG = 1e30
PIECE = 1024
RING = 4

QKV0 = PAIRS * 12
WO = 4 * 8
UPG = FF // 512
UP = UPG * 16
DN = 4 * (FT // 2)
BASE_L1 = QKV0 + WO + UP + DN
L1_QI0 = BASE_L1
L1_KI = L1_QI0 + 4
L1_QI = L1_KI + 4
L1_V = L1_QI + 4 * (PAIRS - 1)
L1_K = L1_V + 8
L1_Q = L1_K + 8
BASE_WO = (QKV0, L1_Q + 4 * PAIRS)
NPIECES = BASE_WO[1] + WO + UP + DN
GROUPS = 4 + 2 * UPG + 4

V_GAIN = 0
V_CONV = 4 * KT
V_DSA = V_CONV + 2 * UPG * 32
NV = V_DSA + 3
C_TRI, C_ONE, C_AVG, C_ID, C_SBM, C_CM, C_COS, C_SIN = 0, 128, 256, 384, 512, 640, 1024, 1280
NC = 1536


def build(nc, x_in, w_all, vecs_in, consts_in, out):
    with ExitStack() as ctx:
        def sb(name, shape, dt=F32, to=ctx):
            return to.enter_context(nc.sbuf_tensor(name, shape, dt))

        def sem(name):
            return ctx.enter_context(nc.semaphore(name))

        psum = ctx.enter_context(nc.psum_tensor("psum", [P, 8, 512], F32))

        raw = sb("raw", [P, RING, PIECE])
        w_hi = sb("w_hi", [P, RING, PIECE], F32R)
        w_lo = sb("w_lo", [P, RING, PIECE], F32R)
        xres = sb("xres", [P, KT, T])
        xg = sb("xg", [P, KT, 2 * T], F32R)
        vecs = sb("vecs", [P, NV + 1])
        avg_d = sb("avg_d", [P, P])
        rs = sb("rs", [P, T + 2])
        part = sb("part", [P, 4, T])
        upad = sb("upad", [P, 4, T + 2])
        conv = sb("conv", [P, 4, T])
        gates = sb("gates", [P, 4, T])

        with ExitStack() as mlp:
            hid = sb("hid", [P, FT, 2 * T], F32R, mlp)
        att_ctx = ctx.enter_context(ExitStack())
        att = sb("att", [P, NH, 2 * T], F32R, att_ctx)
        cst = sb("cst", [P, NC], F32, att_ctx)
        idr = sb("idr", [P, P], F32R, att_ctx)
        with ExitStack() as l0:
            sbm_r = sb("sbm_r", [P, P], F32R, l0)
            rsq = sb("rsq", [P, T], F32, l0)
            tq = sb("tq", [P, 2, T], F32, l0)
            tk = sb("tk", [P, 2, T], F32, l0)
            q0 = sb("q0", [P, 2, T], F32, l0)
            k0 = sb("k0", [P, 2, T], F32, l0)
            q_hl = sb("q_hl", [P, 2, 2, T], F32R, l0)
            k_hl = sb("k_hl", [P, 2, 2, T], F32R, l0)
            v_hl = sb("v_hl", [P, 2, 2, T], F32R, l0)
            sp_hl = sb("sp_hl", [P, 2, 2, 384], F32R, l0)
            aw_hl = sb("aw_hl", [P, 2, 2, 384], F32R, l0)
            tri_r = sb("tri_r", [P, P], F32R, l0)
            neg_r = sb("neg_r", [P, P], F32R, l0)
            az = sb("az", [P, 2, 384], F32, l0)
            sp = sb("sp", [P, 2, 384], F32, l0)
            aw = sb("aw", [P, 2, 384], F32, l0)
        l1 = att_ctx
        v_all = sb("v_all", [P, 2, 512], F32, l1)
        v_cur = sb("v_cur", [P, 2, P], F32, l1)
        k_all = sb("k_all", [P, KVH, T], F32, l1)
        ki = sb("ki", [P, T], F32, l1)
        tu = sb("tu", [P, 2, T], F32, l1)
        usq = sb("usq", [P, 2, T], F32, l1)
        rsn = sb("rsn", [P, 2, T], F32, l1)
        ra = sb("ra", [P, 2, T], F32, l1)
        rb = sb("rb", [P, 2, T], F32, l1)
        qr = sb("qr", [P, 2, T], F32, l1)
        rl = sb("rl", [P, 2, 384], F32, l1)
        score = sb("score", [P, 384], F32, l1)
        work = sb("work", [P, 384], F32, l1)
        cum = sb("cum", [P, 384], F32, l1)
        ones = sb("ones", [P, 256], F32, l1)
        top8 = sb("top8", [P, 2, 8], F32, l1)
        tk_n = sb("tk_n", [P, 2, 2], F32, l1)
        selm = sb("selm", [P, 384], F32R, l1)
        cmask2 = sb("cmask2", [P, 384], F32, l1)
        pr = sb("pr", [P, 2, 384], F32, l1)
        prt = sb("prt", [P, 2, 384], F32, l1)
        mx = sb("mx", [P, 2, 2], F32, l1)
        nmx = sb("nmx", [P, 2, 2], F32, l1)
        sums = sb("sums", [P, 2, 2], F32, l1)
        rc = sb("rc", [P, 2, 2], F32, l1)
        rope_c = sb("rope_c", [P, 3, T], F32, l1)
        rope_s = sb("rope_s", [P, 3, T], F32, l1)
        wi_t = sb("wi_t", [P, T], F32, l1)
        wi_s = sb("wi_s", [P, 2, NH], F32, l1)
        rcs = sb("rcs", [P, 2], F32, l1)

        raw_full = [sem(f"raw_full{s}") for s in range(RING)]
        hi_ready, lo_ready, piece_used = sem("hi_ready"), sem("lo_ready"), sem("piece_used")
        gains_in, vecs_in_s, avg_in, cst_in = sem("gains_loaded"), sem("vecs_loaded"), sem("avg_loaded"), sem("cst_loaded")
        x_loaded = [sem(f"x_loaded{g}") for g in range(4)]
        stored, pads_zero, ones_set = sem("stored"), sem("pads_zero"), sem("ones_set")
        acc_free, b_copied = sem("acc_free"), sem("b_copied")
        x_ready, sq_ready, sqsum_ready = sem("x_ready"), sem("sq_ready"), sem("sqsum_ready")
        xhi_ready, xg_ready = sem("xhi_ready"), sem("xg_ready")
        stat_ready, root_ready, rs_ready = sem("stat_ready"), sem("root_ready"), sem("rs_ready")
        rsq_ready, id_ready = sem("rsq_ready"), sem("id_ready")
        ub_copied, up_scaled, tap0, tap1, tap2 = sem("ub_copied"), sem("up_scaled"), sem("tap0"), sem("tap1"), sem("tap2")
        silu_ready, gated, h_hi, h_ready = sem("silu_ready"), sem("gated"), sem("h_hi"), sem("h_ready")
        up_sum = sem("up_sum")
        qb_copied, kb_copied, q_sum, k_sum = sem("qb_copied"), sem("kb_copied"), sem("q_sum"), sem("k_sum")
        q_scaled, k_scaled, q_hi, k_hi = sem("q_scaled"), sem("k_scaled"), sem("q_hi"), sem("k_hi")
        q_ready, k_ready, v_hi, v_ready = sem("q_ready"), sem("k_ready"), sem("v_hi"), sem("v_ready")
        sp_sum, sp_hi, aw_exp, aw_hi = sem("sp_sum"), sem("sp_hi"), sem("aw_exp"), sem("aw_hi")
        z_ready, az_ready, e_ready, l_ready, sp_ready = (sem(n) for n in ("z_ready", "az_ready", "e_ready", "l_ready", "sp_ready"))
        la_ready, a_ready, o_ready = sem("la_ready"), sem("a_ready"), sem("o_ready")
        att_hi, att_ready = sem("att_hi"), sem("att_ready")
        v1_ready, vcur_ready = sem("v1_ready"), sem("vcur_ready")
        tables_ready = sem("tables_ready")
        wi_copied, wi_sum, wi_turned, rcs_s, wis_ready = (sem(n) for n in ("wi_copied", "wi_sum", "wi_turned", "rcs_s", "wis_ready"))
        rb_copied, rb_sum, rb_u, rb_sq = sem("rb_copied"), sem("rb_sum"), sem("rb_u"), sem("rb_sq")
        ms_ready, ln_ready, rsn_ready = sem("ms_ready"), sem("ln_ready"), sem("rsn_ready")
        terms, roped, qr_ready = sem("terms"), sem("roped"), sem("qr_ready")
        lg_ready, rl_ready, sc_half, sc_ready = sem("lg_ready"), sem("rl_ready"), sem("sc_half"), sem("sc_ready")
        topk_s = sem("topk_step")
        s_ready, mx_ready, nm_ready, p_ready, rc_ready, pn_ready = (sem(n) for n in ("s_ready", "mx_ready", "nm_ready", "p_ready", "rc_ready", "pn_ready"))
        tr_ready, pt_ready, av_ready = sem("tr_ready"), sem("pt_ready"), sem("av_ready")

        wg = w_all.rearrange("n p k -> p n k")
        tri, neg_one = cst[:, C_TRI:C_TRI + P], cst[:, C_ONE:C_ONE + P]
        avg_h, ident = cst[:, C_AVG:C_AVG + P], cst[:, C_ID:C_ID + P]
        cmask = cst[:, C_CM:C_CM + 384]
        cos_t, sin_t = cst[:, C_COS:C_COS + T], cst[:, C_SIN:C_SIN + T]
        THREE = ((0, 0), (0, 1), (1, 0))
        at, width = (0, 128), (128, 256)

        def f32(ap):
            return ap.bitcast(F32)

        def gain(m, tile):
            return vecs[:, bass.ds(V_GAIN + m * KT + tile, 1)]

        def times(i, n):
            return 0 if i is None else i * n

        block = ctx.enter_context(nc.Block())

        @block.sync
        def _(sp_q):
            for n in range(RING):
                sp_q.dma_start(raw[:, n, :], wg[:, n, :]).then_inc(raw_full[n], 16)
            loops = (NPIECES - RING) // RING
            with sp_q.Fori(0, loops) as i:
                for s in range(RING):
                    sp_q.wait_ge(lo_ready, i * RING + s + 1)
                    sp_q.dma_start(raw[:, s, :], wg[:, bass.ds(i * RING + RING + s, 1), :]).then_inc(raw_full[s], 16)
            for n in range(RING * (loops + 1), NPIECES):
                sp_q.wait_ge(lo_ready, n - RING + 1)
                sp_q.dma_start(raw[:, n % RING, :], wg[:, n, :]).then_inc(raw_full[n % RING], 16)

        @block.gpsimd
        def _(pool):
            pool.memset(upad[:, :, 0:2], 0.0).then_inc(pads_zero, 1)
            for g in range(4):
                pool.wait_ge(x_ready, 12 + g + 1)
                pool.dma_start(out[:, 4 * g:4 * g + 4, :], xres[:, 4 * g:4 * g + 4, :]).then_inc(stored, 16)
            pool.wait_ge(stored, 64)

        @block.scalar
        def _(act):
            def split(c, i=None, per=0):
                if c >= NPIECES:
                    return
                act.wait_ge(raw_full[c % RING], times(i, 16 * per // RING) + 16 * (c // RING + 1))
                if c >= RING or i is not None:
                    act.wait_ge(piece_used, times(i, per) + c - RING + 1)
                act.copy(w_hi[:, c % RING, :], raw[:, c % RING, :]).then_inc(hi_ready, 1)

            def norm(m, g):
                n = 4 * m + g
                if m == 0:
                    split(g)
                    act.wait_ge(x_loaded[g], 16)
                else:
                    act.wait_ge(x_ready, n - 4 + 1)
                for k in range(4):
                    act.activation(xg[:, 4 * g + k, 0:T], xres[:, 4 * g + k, :], ACT.Copy, scale=gain(m, 4 * g + k)).then_inc(xhi_ready, 1)
                if not (m == 0 and g == 0):
                    act.wait_ge(sqsum_ready, n)
                act.activation(conv[:, :, :], xres[:, 4 * g:4 * g + 4, :], ACT.Square).then_inc(sq_ready, 1)

            def root(m, bank):
                act.wait_ge(stat_ready, m + 1)
                act.activation(rs[:, :], psum[:, bank, 0:T + 2], ACT.Sqrt, bias=eps_ap).then_inc(root_ready, 1)

            def copy_b(group, bank0, last_piece):
                act.wait_ge(piece_used, last_piece + 1)
                if group:
                    act.wait_ge(x_ready, group)
                act.copy(part[:, :, :], psum[:, bank0:bank0 + 4, T:2 * T]).then_inc(b_copied, 1)

            def out_groups(base, per, m, e0=0, tail=None, head=None):
                for g in range(4):
                    for e in range(e0 if g == 0 else 0, per):
                        if head and g == 0:
                            head(e)
                        split(base + g * per + e + RING)
                        if tail and g == 0:
                            tail(e)
                        if g and e == 0 and m < 4:
                            norm(m, g - 1)
                    copy_b(4 * (m - 1) + g, 4 * (g % 2), base + g * per + per - 1)

            eps_ap = vecs[:, NV:NV + 1]

            act.dma_start(vecs[:, 0:V_CONV], vecs_in[:, 0:V_CONV]).then_inc(gains_in, 16)
            act.dma_start(xres[:, 0:4, :], x_in[:, 0:4, :]).then_inc(x_loaded[0], 16)
            for g in range(1, 4):
                act.dma_start(xres[:, 4 * g:4 * g + 4, :], x_in[:, 4 * g:4 * g + 4, :]).then_inc(x_loaded[g], 16)
            act.dma_start(avg_d[:, :], consts_in[:, NC:NC + P]).then_inc(avg_in, 16)
            act.dma_start(vecs[:, V_CONV:], vecs_in[:, V_CONV:]).then_inc(vecs_in_s, 16)
            act.dma_start(cst[:, :], consts_in[:, 0:NC]).then_inc(cst_in, 16)
            act.preload_act_table_set("natural_log_exp_and_others")
            for g in range(4):
                if g == 0:
                    act.wait_ge(gains_in, 16)
                norm(0, g)

            def l0_ab(j):
                act.wait_ge(la_ready, j + 1)
                if not isinstance(j, int) or j > 0:
                    act.wait_ge(a_ready, j)
                act.activation(aw[:, :, :], psum[:, 5:7, 0:384], ACT.Exp).then_inc(aw_exp, 1)
                act.wait_ge(aw_exp, j + 1)
                if not isinstance(j, int) or j > 0:
                    act.wait_ge(o_ready, j)
                act.copy(aw_hl[:, :, 0, :], aw[:, :, :]).then_inc(aw_hi, 1)

            def l0_out(j):
                act.wait_ge(o_ready, j + 1)
                act.copy(att[:, bass.ds(2 * j, 2), 0:T], psum[:, 7, :].rearrange("p (h t) -> p h t", h=2)).then_inc(att_hi, 1)

            def l0_pair(j, i, per, first):
                for e in range(12):
                    split((0 if i is not None else 12 * j) + e + RING, i, per)
                    n0 = 12 * j
                    if e == 1 and not first:
                        l0_ab(j - 1)
                    if e == 2 and first:
                        root(0, 7)
                        act.preload_act_table_set("natural_log_exp_and_others")
                    if e == 3 and not first:
                        l0_out(j - 1)
                    if e == 3:
                        act.wait_ge(piece_used, n0 + 4)
                        if not first:
                            act.wait_ge(q_ready, j)
                        act.copy(tq[:, :, :], psum[:, 0:2, T:2 * T]).then_inc(qb_copied, 1)
                    if e == 7:
                        act.wait_ge(piece_used, n0 + 8)
                        if not first:
                            act.wait_ge(k_ready, j)
                        act.copy(tk[:, :, :], psum[:, 2:4, T:2 * T]).then_inc(kb_copied, 1)
                    for at_e, scaled, src, dst, done in ((4, q_scaled, q0, q_hl, q_hi), (8, k_scaled, k0, k_hl, k_hi)):
                        if e == at_e:
                            act.wait_ge(scaled, j + 1)
                            if not first:
                                act.wait_ge(z_ready, j)
                            act.copy(dst[:, :, 0, :], src[:, :, :]).then_inc(done, 1)
                    if e == 9:
                        act.wait_ge(z_ready, j + 1)
                        if not first:
                            act.wait_ge(sp_sum, j)
                        act.activation(az[:, :, :], psum[:, 5:7, 0:384], ACT.Abs).then_inc(az_ready, 1)
                        act.wait_ge(az_ready, j + 1)
                        act.activation(az[:, :, :], az[:, :, :], ACT.Exp, scale=-1.0).then_inc(e_ready, 1)
                        act.wait_ge(e_ready, j + 1)
                        act.activation(az[:, :, :], az[:, :, :], ACT.Ln, bias=1.0).then_inc(l_ready, 1)
                    if e == 11:
                        act.wait_ge(sp_sum, j + 1)
                        if not first:
                            act.wait_ge(la_ready, j)
                        act.copy(sp_hl[:, :, 0, :], sp[:, :, :]).then_inc(sp_hi, 1)
                        act.wait_ge(piece_used, n0 + 12)
                        if not first:
                            act.wait_ge(o_ready, j)
                        act.wait_ge(rs_ready, 1)
                        for st in range(2):
                            last = act.activation(v_hl[:, st, 0, :], psum[:, 4, st * T:(st + 1) * T], ACT.Copy, scale=rs[:, T + st:T + st + 1])
                        last.then_inc(v_hi, 1)

            act.wait_ge(cst_in, 16)
            act.copy(idr[:, :], ident)
            act.copy(tri_r[:, :], tri)
            act.copy(neg_r[:, :], neg_one)
            act.copy(sbm_r[:, :], cst[:, C_SBM:C_SBM + P]).then_inc(id_ready, 1)
            l0_pair(0, None, 0, True)
            with act.Fori(1, PAIRS) as i:
                l0_pair(i, i, 12, False)

            def l0_tail(e):
                if e == 1:
                    l0_ab(PAIRS - 1)
                if e == 3:
                    l0_out(PAIRS - 1)
            out_groups(BASE_WO[0], 8, 1, 0, l0_tail)

            def conv_scalars(layer, i, val, k, j):
                return vecs[:, bass.ds(V_CONV + layer * UPG * 32 + times(i, 32) + val * 16 + k * 4 + j, 1)]

            def up_slot(layer, i, e, base):
                val = int(e >= 15)
                u = 2 * UPG * layer + 2 * i + val
                f = UPG * layer + i
                if e in (7, 15):
                    act.wait_ge(piece_used, base + 16 * i + e + 1)
                    act.copy(part[:, :, :], psum[:, 4 * val:4 * val + 4, T:2 * T]).then_inc(ub_copied, 1)
                if e in (8, 16):
                    act.wait_ge(up_scaled, u + 1)
                    for k in range(4):
                        last = act.activation(conv[:, k, :], upad[:, k, 0:T], ACT.Identity,
                                              scale=conv_scalars(layer, i, val, k, 0), bias=conv_scalars(layer, i, val, k, 3))
                    last.then_inc(tap0, 1)
                if e == 10:
                    act.wait_ge(tap2, u + 1)
                    act.activation(gates[:, :, :], conv[:, :, :], ACT.Silu).then_inc(silu_ready, 1)
                if e == 19:
                    act.wait_ge(gated, f + 1)
                    act.copy(hid[:, bass.ds(4 * i, 4), 0:T], gates[:, :, :]).then_inc(h_hi, 1)

            def mlp_layer(layer):
                base = BASE_WO[layer] + WO
                m = 1 + 2 * layer
                for e in range(7):
                    split(base + e + RING)
                    if e == 0:
                        norm(m, 3)
                    if e == 4:
                        root(m, 4)
                        act.preload_act_table_set("silu_and_others")
                if layer == 0:
                    act.wait_ge(vecs_in_s, 16)
                with act.Fori(0, UPG) as i:
                    for e in range(7, 23):
                        split(base + e + RING, i, 16)
                        up_slot(layer, i, e, base)
                out_groups(base + UP, FT // 2, 2 + 2 * layer, 7)

            mlp_layer(0)

            act.dma_start(cst[:, :], consts_in[:, 0:NC]).then_inc(cst_in, 16)
            def evac(B, bank0, nh, last_piece, nb):
                act.wait_ge(piece_used, last_piece + 1)
                if not (isinstance(B, int) and B == 0):
                    act.wait_ge(qr_ready, B)
                act.copy(tu[:, 0:nh, :], psum[:, bank0:bank0 + nh, T:2 * T]).then_inc(rb_copied, 1)
                if nb is not None:
                    act.wait_ge(rb_u, nb + 1)
                    act.activation(usq[:, 0:nh, :], tu[:, 0:nh, :], ACT.Square).then_inc(rb_sq, 1)

            def norm_scale(nh, nb):
                act.wait_ge(ms_ready, nb + 1)
                act.activation(rsn[:, 0:nh, :], psum[:, 5, 0:nh * T].rearrange("p (h t) -> p h t", h=nh), ACT.Ln, bias=eps_ap).then_inc(ln_ready, 1)
                act.wait_ge(ln_ready, nb + 1)
                act.activation(rsn[:, 0:nh, :], rsn[:, 0:nh, :], ACT.Exp, scale=-0.5).then_inc(rsn_ready, 1)

            def relu(t):
                act.wait_ge(lg_ready, t + 1)
                act.wait_ge(sc_ready, t + 1)
                act.activation(rl[:, :, :], psum[:, 6:8, 0:384], ACT.Relu).then_inc(rl_ready, 1)

            def exps(t):
                act.wait_ge(nm_ready, t + 1)
                for h in range(2):
                    for th in range(2):
                        c = slice(at[th], at[th] + width[th])
                        last = act.activation(pr[:, h, c], psum[:, 6 + h, c], ACT.Exp, bias=nmx[:, th, h:h + 1], scale=ATT_SCALE,
                                              accum_out=sums[:, th, h:h + 1])
                last.then_inc(p_ready, 1)

            def prt_copy(t):
                act.wait_ge(tr_ready, t + 1)
                act.copy(prt[:, :, :], psum[:, 6:8, 0:384]).then_inc(pt_ready, 1)

            def out_hi(t):
                act.wait_ge(av_ready, t + 1)
                act.copy(att[:, bass.ds(2 * t, 2), 0:T], psum[:, 4, :].rearrange("p (h t) -> p h t", h=2)).then_inc(att_hi, 1)

            def set_v(g):
                act.copy(v_cur[:, :, :], v_all[:, :, bass.ds(g * P, P)]).then_inc(vcur_ready, 1)

            for e in range(4):
                split(L1_QI0 + e + RING)
                if e == 0:
                    norm(2, 3)
                    act.wait_ge(cst_in, 32)
                    act.copy(idr[:, :], ident).then_inc(id_ready, 1)
            evac(0, 0, 2, L1_QI0 + 3, None)
            for e in range(4):
                split(L1_KI + e + RING)
                if e == 0:
                    root(2, 4)
                    act.preload_act_table_set("natural_log_exp_and_others")
                if e == 1:
                    evac(1, 2, 1, L1_KI + 1, 0)
            act.wait_ge(piece_used, L1_KI + 4)
            act.copy(wi_t[:, :], psum[:, 3, T:2 * T]).then_inc(wi_copied, 1)

            def block1(B, i, per, par, nb, prev_norm, t_relu, t_soft, t_av, base, v_g=None):
                for e in range(4):
                    if e == 0 and v_g is not None:
                        set_v(v_g)
                    if e == 0 and t_soft is not None:
                        exps(t_soft)
                    if e == 0 and t_relu is not None:
                        relu(t_relu)
                    split(base + e + RING, i, per)
                    if e == 1 and prev_norm is not None:
                        norm_scale(prev_norm[1], prev_norm[0])
                    if e == 2 and t_soft is not None:
                        prt_copy(t_soft)
                    if e == 3:
                        evac(B, 2 * par, 2, base + times(i, per) + 3, nb)
                        if t_av is not None:
                            out_hi(t_av)

            block1(2, None, 0, 0, None, (0, 1), None, None, None, L1_QI)
            with act.Fori(0, 3) as i:
                block1(3 + 2 * i, i, 8, 1, None, None, 2 * i, None, None, L1_QI + 4)
                block1(4 + 2 * i, i, 8, 0, None, None, 2 * i + 1, None, None, L1_QI + 8)
            for e in range(8):
                if e % 4 == 0:
                    relu(6 + e // 4)
                split(L1_V + e + RING)
            act.wait_ge(piece_used, L1_V + 8)
            for st in range(2):
                last = act.activation(v_all[:, st, :], psum[:, 2 + st, :], ACT.Copy, scale=rs[:, T + st:T + st + 1])
            last.then_inc(v1_ready, 1)
            block1(9, None, 0, 0, 1, None, None, None, None, L1_K)
            block1(10, None, 0, 1, 2, (1, 2), None, None, None, L1_K + 4)
            block1(11, None, 0, 0, 3, (2, 2), None, None, None, L1_Q)
            block1(12, None, 0, 1, 4, (3, 2), None, None, None, L1_Q + 4)
            with act.Fori(0, 3) as i:
                block1(13 + 2 * i, i, 8, 0, 5 + 2 * i, (4 + 2 * i, 2), None, 2 * i, 2 * i, L1_Q + 8, v_g=i)
                block1(14 + 2 * i, i, 8, 1, 6 + 2 * i, (5 + 2 * i, 2), None, 2 * i + 1, 2 * i + 1, L1_Q + 12)

            def l1_head(e):
                if e == 0:
                    set_v(3)
                    exps(6)
                if e == 3:
                    exps(7)

            def l1_tail(e):
                if e == 1:
                    norm_scale(2, 10)
                    prt_copy(6)
                if e == 2:
                    out_hi(6)
                if e == 4:
                    prt_copy(7)
                if e == 5:
                    out_hi(7)
            out_groups(BASE_WO[1], 8, 3, 0, l1_tail, l1_head)
            mlp_layer(1)

        @block.vector
        def _(dve):
            def split(c, i=None, per=0):
                if c >= NPIECES:
                    return
                dve.wait_ge(hi_ready, times(i, per) + c + 1)
                dve.tensor_tensor(w_lo[:, c % RING, :], raw[:, c % RING, :], f32(w_hi[:, c % RING, :]), ALU.subtract).then_inc(lo_ready, 1)

            def norm(m, g):
                n = 4 * m + g
                if m == 0:
                    split(g)
                for k in range(4):
                    dve.wait_ge(xhi_ready, 4 * n + k + 1)
                    last = dve.scalar_tensor_tensor(out=xg[:, 4 * g + k, T:2 * T], in0=xres[:, 4 * g + k, :], scalar=gain(m, 4 * g + k),
                                                    in1=f32(xg[:, 4 * g + k, 0:T]), op0=ALU.mult, op1=ALU.subtract)
                last.then_inc(xg_ready, 1)
                dve.wait_ge(sq_ready, n + 1)
                dve.tensor_reduce(gates[:, g, :], conv[:, :, :].rearrange("p k t -> p t k"), AX.X, ALU.add).then_inc(sqsum_ready, 1)

            def recip(m):
                dve.wait_ge(root_ready, m + 1)
                dve.reciprocal(rs[:, :], rs[:, :]).then_inc(rs_ready, 1)

            def add_group(o, g, bank0):
                dve.wait_ge(b_copied, o + 1)
                dve.tensor_tensor(part[:, :, :], psum[:, bank0:bank0 + 4, 0:T], part[:, :, :], ALU.add).then_inc(acc_free, 1)
                dve.wait_ge(acc_free, GROUPS * (o // 8) + (4 + 2 * UPG) * (o // 4 % 2) + g + 1)
                dve.tensor_tensor(xres[:, 4 * g:4 * g + 4, :], xres[:, 4 * g:4 * g + 4, :], part[:, :, :], ALU.add).then_inc(x_ready, 1)

            def out_groups(base, per, m, e0=0, tail=None, head=None):
                for g in range(4):
                    for e in range(e0 if g == 0 else 0, per):
                        if head and g == 0:
                            head(e)
                        split(base + g * per + e + RING)
                        if tail and g == 0:
                            tail(e)
                        if g and e == 1 and m < 4:
                            norm(m, g - 1)
                    add_group(4 * (m - 1) + g, g, 4 * (g % 2))

            dve.wait_ge(gains_in, 16)
            for g in range(4):
                norm(0, g)

            def l0_out(j):
                dve.wait_ge(att_hi, j + 1)
                dst = att[:, bass.ds(2 * j, 2), :]
                dve.tensor_tensor(dst[:, :, T:2 * T], psum[:, 7, :].rearrange("p (h t) -> p h t", h=2), f32(dst[:, :, 0:T]),
                                  ALU.subtract).then_inc(att_ready, 1)

            def l0_aw_lo(j):
                dve.wait_ge(aw_hi, j + 1)
                dve.tensor_tensor(aw_hl[:, :, 1, :], aw[:, :, :], f32(aw_hl[:, :, 0, :]), ALU.subtract).then_inc(a_ready, 1)

            def over_heads(ap, n=2):
                return ap.unsqueeze(1).to_broadcast([P, n, T])

            def l0_pair(j, i, per, first):
                n0 = None if i is not None else 12 * j
                for e in range(12):
                    split((0 if i is not None else 12 * j) + e + RING, i, per)
                    if e == 2 and first:
                        recip(0)
                        dve.wait_ge(rs_ready, 1)
                        dve.tensor_scalar(rsq[:, :], rs[:, 0:T], ATT_SCALE, None, ALU.mult).then_inc(rsq_ready, 1)
                        dve.wait_ge(rsq_ready, 1)
                    if e == 1 and not first:
                        l0_aw_lo(j - 1)
                    if e == 3 and not first:
                        l0_out(j - 1)
                    for at_e, b_done, tmp, summed, scale, dst, done, bank in (
                            (3, qb_copied, tq, q_sum, rsq[:, :], q0, q_scaled, 0), (7, kb_copied, tk, k_sum, rs[:, 0:T], k0, k_scaled, 2)):
                        if e == at_e:
                            dve.wait_ge(b_done, j + 1)
                            dve.tensor_tensor(tmp[:, :, :], psum[:, bank:bank + 2, 0:T], tmp[:, :, :], ALU.add).then_inc(summed, 1)
                            dve.wait_ge(summed, j + 1)
                            dve.tensor_tensor(dst[:, :, :], tmp[:, :, :], over_heads(scale), ALU.mult).then_inc(done, 1)
                    for at_e, hi, src, dst, done in ((5, q_hi, q0, q_hl, q_ready), (8, k_hi, k0, k_hl, k_ready)):
                        if e == at_e:
                            dve.wait_ge(hi, j + 1)
                            dve.tensor_tensor(dst[:, :, 1, :], src[:, :, :], f32(dst[:, :, 0, :]), ALU.subtract).then_inc(done, 1)
                    if e == 10:
                        dve.wait_ge(l_ready, j + 1)
                        dve.scalar_tensor_tensor(out=sp[:, :, :], in0=psum[:, 5:7, 0:384], scalar=0.0, in1=az[:, :, :],
                                                 op0=ALU.max, op1=ALU.add).then_inc(sp_sum, 1)
                    if e == 11:
                        dve.wait_ge(sp_hi, j + 1)
                        dve.tensor_tensor(sp_hl[:, :, 1, :], sp[:, :, :], f32(sp_hl[:, :, 0, :]), ALU.subtract).then_inc(sp_ready, 1)
                        dve.wait_ge(v_hi, j + 1)
                        for st in range(2):
                            last = dve.scalar_tensor_tensor(out=v_hl[:, st, 1, :], in0=psum[:, 4, st * T:(st + 1) * T], scalar=rs[:, T + st:T + st + 1],
                                                            in1=f32(v_hl[:, st, 0, :]), op0=ALU.mult, op1=ALU.subtract)
                        last.then_inc(v_ready, 1)

            l0_pair(0, None, 0, True)
            with dve.Fori(1, PAIRS) as i:
                l0_pair(i, i, 12, False)

            def l0_tail(e):
                if e == 1:
                    l0_aw_lo(PAIRS - 1)
                if e == 3:
                    l0_out(PAIRS - 1)
            out_groups(BASE_WO[0], 8, 1, 0, l0_tail)

            def conv_scalars(layer, i, val, k, j):
                return vecs[:, bass.ds(V_CONV + layer * UPG * 32 + times(i, 32) + val * 16 + k * 4 + j, 1)]

            def up_slot(layer, i, e):
                val = int(e >= 15)
                u = 2 * UPG * layer + 2 * i + val
                f = UPG * layer + i
                if e in (7, 15):
                    dve.wait_ge(ub_copied, u + 1)
                    dve.tensor_tensor(part[:, :, :], psum[:, 4 * val:4 * val + 4, 0:T], part[:, :, :], ALU.add).then_inc(acc_free, 1)
                    dve.wait_ge(acc_free, GROUPS * layer + 4 + 2 * i + val + 1)
                    dve.tensor_tensor(upad[:, :, 2:T + 2], part[:, :, :], over_heads(rs[:, 0:T], 4), ALU.mult).then_inc(up_scaled, 1)
                if e in (9, 17):
                    dve.wait_ge(tap0, u + 1)
                    for j, done in ((1, tap1), (2, tap2)):
                        for k in range(4):
                            last = dve.scalar_tensor_tensor(out=conv[:, k, :], in0=upad[:, k, j:j + T], scalar=conv_scalars(layer, i, val, k, j),
                                                            in1=conv[:, k, :], op0=ALU.mult, op1=ALU.add)
                        last.then_inc(done, 1)
                        dve.wait_ge(done, u + 1)
                if e == 18:
                    dve.wait_ge(silu_ready, f + 1)
                    dve.tensor_tensor(gates[:, :, :], gates[:, :, :], conv[:, :, :], ALU.mult).then_inc(gated, 1)
                if e == 20:
                    dve.wait_ge(h_hi, f + 1)
                    dst = hid[:, bass.ds(4 * i, 4), :]
                    dve.tensor_tensor(dst[:, :, T:2 * T], gates[:, :, :], f32(dst[:, :, 0:T]), ALU.subtract).then_inc(h_ready, 1)

            def mlp_layer(layer):
                base = BASE_WO[layer] + WO
                m = 1 + 2 * layer
                if layer == 0:
                    dve.wait_ge(pads_zero, 1)
                    dve.wait_ge(vecs_in_s, 16)
                for e in range(7):
                    if e == 1:
                        norm(m, 3)
                    split(base + e + RING)
                    if e == 4:
                        recip(m)
                        dve.wait_ge(rs_ready, m + 1)
                with dve.Fori(0, UPG) as i:
                    for e in range(7, 23):
                        split(base + e + RING, i, 16)
                        up_slot(layer, i, e)
                out_groups(base + UP, FT // 2, 2 + 2 * layer, 7)

            mlp_layer(0)

            def evac(B, bank0, nh, nb):
                dve.wait_ge(rb_copied, B + 1)
                dve.tensor_tensor(tu[:, 0:nh, :], psum[:, bank0:bank0 + nh, 0:T], tu[:, 0:nh, :], ALU.add).then_inc(rb_sum, 1)
                if nb is not None:
                    dve.wait_ge(rb_sum, B + 1)
                    dve.tensor_tensor(tu[:, 0:nh, :], tu[:, 0:nh, :], over_heads(rs[:, 0:T], nh), ALU.mult).then_inc(rb_u, 1)

            def rope(B, nh, nb, c_t, s_t, dst, after=None, parts=(0, 1)):
                if 0 in parts:
                    if nb is None:
                        dve.wait_ge(rb_sum, B + 1)
                    else:
                        dve.wait_ge(rb_u, nb + 1)
                    dve.tensor_tensor(ra[:, 0:nh, :], tu[:, 0:nh, :], over_heads(c_t, nh), ALU.mult)
                    for lo, hi in ((0, P // 2), (P // 2, 0)):
                        last = dve.tensor_tensor(rb[hi:hi + P // 2, 0:nh, :], tu[lo:lo + P // 2, 0:nh, :],
                                                 s_t[lo:lo + P // 2, :].unsqueeze(1).to_broadcast([P // 2, nh, T]), ALU.mult)
                    last.then_inc(terms, 1)
                    dve.wait_ge(terms, B + 1)
                    if nb is not None:
                        dve.tensor_tensor(ra[:, 0:nh, :], ra[:, 0:nh, :], rb[:, 0:nh, :], ALU.add).then_inc(roped, 1)
                if 1 in parts:
                    if after is not None:
                        dve.wait_ge(*after)
                    if nb is None:
                        dve.tensor_tensor(dst, ra[:, 0:nh, :], rb[:, 0:nh, :], ALU.add).then_inc(qr_ready, 1)
                    else:
                        dve.wait_ge(roped, nb + 1)
                        dve.wait_ge(rsn_ready, nb + 1)
                        dve.tensor_tensor(dst, ra[:, 0:nh, :], rsn[:, 0:nh, :], ALU.mult).then_inc(qr_ready, 1)

            def rope_prev(B, kind, nb=None, parts=(0, 1)):
                if kind == "ki":
                    rope(B, 1, nb, rope_c[:, 2, :], rope_s[:, 2, :], ki[:, :].unsqueeze(1))
                elif kind == "qi":
                    first = isinstance(B, int) and B == 0
                    rope(B, 2, None, cos_t, sin_t, qr[:, :, :], None if first else (lg_ready, B - 1))
                elif kind == "k":
                    rope(B, 2, nb, rope_c[:, 1, :], rope_s[:, 1, :], k_all[:, 2 * (B - 9):2 * (B - 9) + 2, :])
                else:
                    after = (lg_ready, 8) if isinstance(B, int) and B == 11 else (s_ready, B - 11)
                    rope(B, 2, nb, rope_c[:, 0, :], rope_s[:, 0, :], qr[:, :, :], after, parts)

            def add_scores(t):
                dve.wait_ge(rl_ready, t + 1)
                for h in range(2):
                    dve.wait_ge(sc_half if h else sc_ready, t + 1)
                    for th in range(2):
                        c = slice(at[th], at[th] + width[th])
                        last = dve.scalar_tensor_tensor(out=score[:, c], in0=rl[:, h, c], scalar=wi_s[:, th, bass.ds(2 * t + h, 1)],
                                                        in1=score[:, c], op0=ALU.mult, op1=ALU.add)
                    last.then_inc(sc_ready if h else sc_half, 1)

            step = [0]

            def both(op):
                for th in (1, 0):
                    if step[0] >= 2:
                        dve.wait_ge(topk_s, step[0] - 1)
                    op(th, slice(at[th], at[th] + width[th])).then_inc(topk_s, 1)
                    step[0] += 1

            def mask_scores():
                dve.wait_ge(sc_ready, PAIRS + 1)
                both(lambda th, c: dve.tensor_tensor(score[:, c], score[:, c], cmask[:, c], ALU.add))
                both(lambda th, c: dve.tensor_copy(work[:, c], score[:, c]))

            def top_rounds(lo, hi):
                for r in range(lo, hi):
                    both(lambda th, c: dve.max(top8[:, th, :], work[:, c]))
                    if r < TOPK // 8 - 1:
                        both(lambda th, c: dve.match_replace(work[:, c], top8[:, th, :], work[:, c], -3e38))

            def select(part):
                thr = top8[:, :, 7:8]
                if part == 0:
                    both(lambda th, c: dve.tensor_scalar(work[:, c], score[:, c], thr[:, th, :], None, ALU.is_gt))
                    both(lambda th, c: dve.tensor_reduce(tk_n[:, th, 0:1], work[:, c], AX.X, ALU.add))
                    both(lambda th, c: dve.tensor_scalar(tk_n[:, th, 1:2], tk_n[:, th, 0:1], -1.0, float(TOPK), ALU.mult, ALU.add))
                    both(lambda th, c: dve.tensor_scalar(score[:, c], score[:, c], thr[:, th, :], None, ALU.is_equal))
                else:
                    both(lambda th, c: dve.tensor_tensor_scan(cum[:, c], ones[:, 0:width[th]], score[:, c], 0.0, ALU.mult, ALU.add))
                    both(lambda th, c: dve.scalar_tensor_tensor(out=score[:, c], in0=cum[:, c], scalar=tk_n[:, th, 1:2], in1=score[:, c],
                                                                op0=ALU.is_le, op1=ALU.mult))
                    both(lambda th, c: dve.tensor_tensor(work[:, c], work[:, c], score[:, c], ALU.add))
                    both(lambda th, c: dve.scalar_tensor_tensor(out=selm[:, c], in0=work[:, c], scalar=BIG, in1=cmask2[:, c],
                                                                op0=ALU.mult, op1=ALU.add))

            def maxes(t):
                dve.wait_ge(s_ready, t + 1)
                for th in range(2):
                    last = dve.tensor_reduce(mx[:, th, :], psum[:, 6:8, at[th]:at[th] + width[th]], AX.X, ALU.max)
                last.then_inc(mx_ready, 1)
                dve.wait_ge(mx_ready, t + 1)
                dve.tensor_scalar(nmx[:, :, :], mx[:, :, :], -ATT_SCALE, None, ALU.mult).then_inc(nm_ready, 1)

            def normalise(t):
                dve.wait_ge(p_ready, t + 1)
                dve.reciprocal(rc[:, :, :], sums[:, :, :]).then_inc(rc_ready, 1)
                dve.wait_ge(rc_ready, t + 1)
                for h in range(2):
                    for th in range(2):
                        c = slice(at[th], at[th] + width[th])
                        last = dve.tensor_scalar(pr[:, h, c], pr[:, h, c], rc[:, th, h:h + 1], None, ALU.mult)
                last.then_inc(pn_ready, 1)

            def out_lo(t):
                dve.wait_ge(att_hi, PAIRS + t + 1)
                dst = att[:, bass.ds(2 * t, 2), :]
                dve.tensor_tensor(dst[:, :, T:2 * T], psum[:, 4, :].rearrange("p (h t) -> p h t", h=2), f32(dst[:, :, 0:T]),
                                  ALU.subtract).then_inc(att_ready, 1)

            def index_weights():
                dve.wait_ge(wi_turned, 1)
                dve.wait_ge(rcs_s, 1)
                for th in range(2):
                    last = dve.tensor_scalar(wi_s[:, th, :], psum[:, 4, th * P:th * P + NH], rs[:, T + th:T + th + 1], rcs[:, th:th + 1],
                                             ALU.mult, ALU.mult)
                last.then_inc(wis_ready, 1)
                dve.wait_ge(wis_ready, 1)

            for e in range(4):
                if e == 1:
                    norm(2, 3)
                split(L1_QI0 + e + RING)
                if e == 2:
                    dve.wait_ge(cst_in, 32)
                    for n in range(3):
                        dve.tensor_scalar(rope_c[:, n, :], cos_t, vecs[:, V_DSA + n:V_DSA + n + 1], None, ALU.mult)
                        last = dve.tensor_scalar(rope_s[:, n, :], sin_t, vecs[:, V_DSA + n:V_DSA + n + 1], None, ALU.mult)
                    last.then_inc(tables_ready, 1)
                    dve.tensor_scalar(cmask2[:, :], cmask, -BIG, None, ALU.add).then_inc(tables_ready, 1)
                    dve.memset(score[:, :], 0.0).then_inc(sc_ready, 1)
                    dve.memset(ones[:, :], 1.0).then_inc(ones_set, 1)
                    dve.wait_ge(ones_set, 1)
                    dve.wait_ge(tables_ready, 2)
            evac(0, 0, 2, None)
            for e in range(4):
                split(L1_KI + e + RING)
                if e == 0:
                    recip(2)
                    dve.wait_ge(rs_ready, 3)
                    dve.tensor_scalar(rcs[:, :], rs[:, T:T + 2], WI_SCALE, None, ALU.mult).then_inc(rcs_s, 1)
                    rope_prev(0, "qi")
                if e == 1:
                    evac(1, 2, 1, 0)
            dve.wait_ge(wi_copied, 1)
            dve.tensor_tensor(wi_t[:, :], psum[:, 3, 0:T], wi_t[:, :], ALU.add).then_inc(wi_sum, 1)

            def block1(B, i, per, par, nb, prev, t_score, t_soft, t_av, base, extra=None):
                for e in range(4):
                    if e == 0 and t_soft is not None:
                        maxes(t_soft)
                        normalise(t_soft)
                    split(base + e + RING, i, per)
                    if e == 0 and t_score is not None:
                        add_scores(t_score)
                    if e == 1 and prev is not None:
                        rope_prev(B - 1, *prev)
                    if e == 3:
                        evac(B, 2 * par, 2, nb)
                        if t_av is not None:
                            out_lo(t_av)
                    if extra is not None:
                        extra(e)

            block1(2, None, 0, 0, None, ("ki", 0), None, None, None, L1_QI, lambda e: index_weights() if e == 2 else None)
            with dve.Fori(0, 3) as i:
                block1(3 + 2 * i, i, 8, 1, None, ("qi",), 2 * i, None, None, L1_QI + 4)
                block1(4 + 2 * i, i, 8, 0, None, ("qi",), 2 * i + 1, None, None, L1_QI + 8)
            for e in range(8):
                split(L1_V + e + RING)
                if e % 4 == 0:
                    add_scores(6 + e // 4)
                if e == 1:
                    rope_prev(8, "qi")
                if e == 4:
                    mask_scores()
                if e >= 5:
                    top_rounds(2 * (e - 5), 2 * (e - 4))

            def topk_a(e):
                if e == 0:
                    top_rounds(6, 8)

            def topk_b(e):
                if e == 0:
                    select(0)

            def topk_c(e):
                if e == 0:
                    select(1)

            block1(9, None, 0, 0, 1, None, None, None, None, L1_K, topk_a)
            block1(10, None, 0, 1, 2, ("k", 1), None, None, None, L1_K + 4, topk_b)
            block1(11, None, 0, 0, 3, ("k", 2), None, None, None, L1_Q, topk_c)
            block1(12, None, 0, 1, 4, ("q", 3), None, None, None, L1_Q + 4)
            with dve.Fori(0, 3) as i:
                block1(13 + 2 * i, i, 8, 0, 5 + 2 * i, ("q", 4 + 2 * i), None, 2 * i, 2 * i, L1_Q + 8)
                block1(14 + 2 * i, i, 8, 1, 6 + 2 * i, ("q", 5 + 2 * i), None, 2 * i + 1, 2 * i + 1, L1_Q + 12)

            def l1_head(e):
                if e in (0, 3):
                    maxes(6 + e // 3)
                    normalise(6 + e // 3)

            def l1_tail(e):
                if e in (0, 1):
                    rope_prev(18, "q", 10, (e,))
                if e == 2:
                    out_lo(6)
                if e == 5:
                    out_lo(7)
            out_groups(BASE_WO[1], 8, 3, 0, l1_tail, l1_head)
            mlp_layer(1)

        @block.tensor
        def _(pe):
            def mm(o, lhsT, rhs, start=False):
                return pe.matmul(o, lhsT, rhs, start=start, stop=True, skip_group_check=True)

            def proj(c, i, per, bank0, act_in, kts, k0_, cols, first):
                pe.wait_ge(lo_ready, times(i, per) + c + 1)
                s = c % RING
                for ct in range(cols // P):
                    for kk in range(kts):
                        w = slice(kk * cols + ct * P, kk * cols + (ct + 1) * P)
                        k = k0_ + kk
                        mm(psum[:, bank0 + ct, :], w_hi[:, s, w], act_in[:, k, :], first and kk == 0)
                        last = mm(psum[:, bank0 + ct, 0:T], w_lo[:, s, w], act_in[:, k, 0:T])
                last.then_inc(piece_used, 1)

            def proj_tokens(c, i, per, places, kts, k0_, cols, first):
                pe.wait_ge(lo_ready, times(i, per) + c + 1)
                s = c % RING
                for kk in range(kts):
                    w = slice(kk * cols, (kk + 1) * cols)
                    for th in range(2):
                        k = k0_ + kk
                        new = first and kk == 0 and places[th][1]
                        x_hi, x_lo = xg[:, k, th * P:(th + 1) * P], xg[:, k, T + th * P:T + (th + 1) * P]
                        mm(places[th][0], x_hi, w_hi[:, s, w], new)
                        mm(places[th][0], x_hi, w_lo[:, s, w])
                        last = mm(places[th][0], x_lo, w_hi[:, s, w])
                last.then_inc(piece_used, 1)

            def stat(m, bank):
                pe.wait_ge(sqsum_ready, 4 * (m + 1))
                if m == 0:
                    pe.wait_ge(avg_in, 16)
                for g in range(4):
                    mm(psum[:, bank, 0:T], avg_d[:, :], gates[:, g, :], g == 0)
                for th in range(2):
                    for g in range(4):
                        last = mm(psum[:, bank, T + th:T + th + 1], gates[:, g, th * P:(th + 1) * P], avg_d[:, 0:1])
                last.then_inc(stat_ready, 1)

            def out_groups(base, layer, per, src, n0, ready, tail=None):
                for g in range(4):
                    n = GROUPS * layer + n0 + g
                    if g >= 2 or n0:
                        pe.wait_ge(acc_free, n - 1)
                    for e in range(per):
                        if g == 0:
                            ready(e)
                        proj(base + g * per + e, None, 0, 4 * (g % 2), src, 2, 2 * e, 512, e == 0)
                        if tail and g == 0:
                            tail(e)

            def l0_logits(j):
                pe.wait_ge(q_ready, j + 1)
                pe.wait_ge(k_ready, j + 1)
                if not (isinstance(j, int) and j == 0):
                    pe.wait_ge(a_ready, j)
                for h in range(2):
                    b = 5 + h
                    for n, (kp, qp) in enumerate(THREE):
                        mm(psum[:, b, 0:T], k_hl[:, h, kp, 0:P], q_hl[:, h, qp, :], n == 0)
                        mm(psum[:, b, T:384], k_hl[:, h, kp, P:T], q_hl[:, h, qp, P:T])
                    mm(psum[:, b, 0:P], idr[:, :], sbm_r[:, :])
                    last = mm(psum[:, b, T:384], idr[:, :], sbm_r[:, :])
                last.then_inc(z_ready, 1)

            def l0_tri(j):
                pe.wait_ge(sp_ready, j + 1)
                for h in range(2):
                    b = 5 + h
                    for part_ in range(2):
                        mm(psum[:, b, 0:T], tri_r[:, :], sp_hl[:, h, part_, 0:T])
                        mm(psum[:, b, P:T], neg_r[:, :], sp_hl[:, h, part_, T:384])
                        last = mm(psum[:, b, T:384], tri_r[:, :], sp_hl[:, h, part_, T:384])
                last.then_inc(la_ready, 1)

            def l0_av(j):
                pe.wait_ge(a_ready, j + 1)
                pe.wait_ge(v_ready, j + 1)
                if not (isinstance(j, int) and j == 0):
                    pe.wait_ge(att_ready, j)
                for h in range(2):
                    for n, (vp, ap) in enumerate(THREE):
                        mm(psum[:, 7, h * T:(h + 1) * T], v_hl[:, 0, vp, h * P:(h + 1) * P], aw_hl[:, h, ap, 0:T], h == 0 and n == 0)
                        last = mm(psum[:, 7, h * T + P:(h + 1) * T], v_hl[:, 1, vp, h * P:(h + 1) * P], aw_hl[:, h, ap, T:384])
                last.then_inc(o_ready, 1)

            def l0_pair(j, i, per, first):
                c0 = 0 if i is not None else 12 * j
                for e in range(12):
                    kind, q = e // 4, e % 4
                    if first and kind == 0:
                        pe.wait_ge(xg_ready, q + 1)
                    if q == 0 and not first:
                        pe.wait_ge((q_ready, k_ready, v_ready)[kind], j)
                    if kind < 2:
                        proj(c0 + e, i, per, 2 * kind, xg, 4, 4 * q, 256, q == 0)
                    else:
                        proj_tokens(c0 + e, i, per, ((psum[:, 4, 0:T], True), (psum[:, 4, T:2 * T], False)), 4, 4 * q, 256, q == 0)
                    if e == 1 and not first:
                        l0_tri(j - 1)
                    if e == 2 and first:
                        stat(0, 7)
                    if e == 3 and not first:
                        l0_av(j - 1)
                    if e == 9:
                        if first:
                            pe.wait_ge(id_ready, 1)
                        l0_logits(j)

            l0_pair(0, None, 0, True)
            with pe.Fori(1, PAIRS) as i:
                l0_pair(i, i, 12, False)

            def l0_tail(e):
                if e == 1:
                    l0_tri(PAIRS - 1)
                if e == 3:
                    l0_av(PAIRS - 1)

            def wo0_ready(e):
                if e == 0:
                    pe.wait_ge(k_ready, PAIRS)
                pe.wait_ge(att_ready, e + 1)
            out_groups(BASE_WO[0], 0, 8, att, 0, wo0_ready, l0_tail)

            def up_body(layer, i, fi, base, m):
                for e in range(16):
                    if e % 8 == 0:
                        pe.wait_ge(acc_free, GROUPS * layer + 3 + 2 * i + e // 8)
                    if m is not None and e < 8 and e % 2 == 0:
                        pe.wait_ge(xg_ready, 4 * m + e // 2 + 1)
                    if m is not None and e == 8:
                        pe.wait_ge(root_ready, m + 1)
                    proj(base + e, fi, 16, 4 * (e // 8), xg, 2, 2 * (e % 8), 512, e % 8 == 0)
                    if m is not None and e == 4:
                        pe.wait_ge(acc_free, GROUPS * layer + 4)
                        stat(m, 4)

            def mlp_layer(layer):
                base = BASE_WO[layer] + WO
                up_body(layer, 0, None, base, 1 + 2 * layer)
                with pe.Fori(1, UPG) as i:
                    up_body(layer, i, i, base, None)
                out_groups(base + UP, layer, FT // 2, hid, 4 + 2 * UPG,
                           lambda e: pe.wait_ge(h_ready, UPG * layer + e // 2 + 1))

            mlp_layer(0)

            def mean_squares(nh, nb):
                pe.wait_ge(rb_sq, nb + 1)
                if not (isinstance(nb, int) and nb == 0):
                    pe.wait_ge(rsn_ready, nb)
                mm(psum[:, 5, 0:nh * T], avg_h, usq[:, 0:nh, :], True).then_inc(ms_ready, 1)

            def turn_wi():
                pe.wait_ge(wi_sum, 1)
                for th in range(2):
                    last = pe.transpose(psum[:, 4, th * P:(th + 1) * P], wi_t[:, th * P:(th + 1) * P], ident)
                last.then_inc(wi_turned, 1)

            def logits(t):
                pe.wait_ge(qr_ready, t + 2)
                if not (isinstance(t, int) and t == 0):
                    pe.wait_ge(rl_ready, t)
                for h in range(2):
                    mm(psum[:, 6 + h, 0:P], qr[:, h, 0:P], ki[:, 0:P], True)
                    last = mm(psum[:, 6 + h, P:384], qr[:, h, P:T], ki[:, :])
                last.then_inc(lg_ready, 1)

            def scores(t, g):
                pe.wait_ge(qr_ready, t + 12)
                if isinstance(t, int) and t == 0:
                    pe.wait_ge(rl_ready, PAIRS)
                    pe.wait_ge(topk_s, TOPK_STEPS)
                else:
                    pe.wait_ge(pt_ready, t)
                for h in range(2):
                    b = 6 + h
                    mm(psum[:, b, 0:P], qr[:, h, 0:P], k_all[:, bass.ds(g, 1), 0:P], True)
                    mm(psum[:, b, P:384], qr[:, h, P:T], k_all[:, bass.ds(g, 1), :])
                    last = mm(psum[:, b, 0:384], idr[:, :], selm[:, :])
                last.then_inc(s_ready, 1)

            def transposes(t):
                pe.wait_ge(pn_ready, t + 1)
                for h in range(2):
                    for o, c in ((0, 0), (1, 1), (2, 2)):
                        last = pe.transpose(psum[:, 6 + h, o * P:(o + 1) * P], pr[:, h, c * P:(c + 1) * P], ident)
                last.then_inc(tr_ready, 1)

            def values(t, n_v):
                pe.wait_ge(pt_ready, t + 1)
                pe.wait_ge(vcur_ready, n_v)
                pe.wait_ge(att_ready, PAIRS + t)
                o = psum[:, 4, :].rearrange("p (h t) -> p h t", h=2)
                mm(o, v_cur[:, 0, :], prt[:, :, 0:T], True)
                mm(o[:, :, P:T], v_cur[:, 1, :], prt[:, :, T:384]).then_inc(av_ready, 1)

            def block1(B, i, per, par, prev_nh, prev_nb, t_log, t_score, g_score, t_tr, n_v, base):
                if isinstance(B, int) and B == 9:
                    pe.wait_ge(rb_sum, 9)
                elif isinstance(B, int) and B == 10:
                    pe.wait_ge(v1_ready, 1)
                else:
                    pe.wait_ge(rb_sum, B - 1)
                for e in range(4):
                    proj(base + e, i, per, 2 * par, xg, 4, 4 * e, 256, e == 0)
                    if e == 1 and prev_nb is not None:
                        mean_squares(prev_nh, prev_nb)
                    if e == 1 and isinstance(B, int) and B == 2:
                        turn_wi()
                    if e == 2 and t_tr is not None:
                        transposes(t_tr)
                    if e == 3:
                        if t_log is not None:
                            logits(t_log)
                        if t_tr is not None:
                            values(t_tr, n_v)
                        if t_score is not None:
                            scores(t_score, g_score)

            pe.wait_ge(acc_free, GROUPS - 1)
            for e in range(4):
                pe.wait_ge(xg_ready, 8 + e + 1)
                proj(L1_QI0 + e, None, 0, 0, xg, 4, 4 * e, 256, e == 0)
            for e in range(4):
                proj(L1_KI + e, None, 0, 2 + e // 2, xg, 8, 8 * (e % 2), P, e % 2 == 0)
                if e == 0:
                    pe.wait_ge(acc_free, GROUPS)
                    stat(2, 4)
            block1(2, None, 0, 0, 1, 0, 0, None, None, None, None, L1_QI)
            with pe.Fori(0, 3) as i:
                block1(3 + 2 * i, i, 8, 1, 2, None, 2 * i + 1, None, None, None, None, L1_QI + 4)
                block1(4 + 2 * i, i, 8, 0, 2, None, 2 * i + 2, None, None, None, None, L1_QI + 8)
            pe.wait_ge(wi_sum, 1)
            pe.wait_ge(rb_sum, 8)
            for e in range(8):
                proj_tokens(L1_V + e, None, 0, ((psum[:, 2, :], True), (psum[:, 3, :], True)), 2, 2 * e, 512, e == 0)
                if e == 3:
                    logits(7)
            block1(9, None, 0, 0, 2, None, None, None, None, None, None, L1_K)
            block1(10, None, 0, 1, 2, 1, None, None, None, None, None, L1_K + 4)
            block1(11, None, 0, 0, 2, 2, None, None, None, None, None, L1_Q)
            block1(12, None, 0, 1, 2, 3, None, 0, 0, None, None, L1_Q + 4)
            with pe.Fori(0, 3) as i:
                block1(13 + 2 * i, i, 8, 0, 2, 4 + 2 * i, None, 2 * i + 1, i, 2 * i, i + 1, L1_Q + 8)
                block1(14 + 2 * i, i, 8, 1, 2, 5 + 2 * i, None, 2 * i + 2, i + 1, 2 * i + 1, i + 1, L1_Q + 12)

            def l1_tail(e):
                if e == 1:
                    mean_squares(2, 10)
                    transposes(6)
                if e == 2:
                    values(6, 4)
                    scores(7, 3)
                if e == 4:
                    transposes(7)
                if e == 5:
                    values(7, 4)

            def wo1_ready(e):
                if e == 0:
                    pe.wait_ge(rb_sum, 19)
                pe.wait_ge(att_ready, PAIRS + e + 1)
            out_groups(BASE_WO[1], 1, 8, att, 0, wo1_ready, l1_tail)
            mlp_layer(1)


def _pieces(w, kts, cols):
    k, n = w.shape
    return w.reshape(k // (P * kts), kts, P, n // cols, cols).transpose(3, 0, 2, 1, 4).reshape(n // cols, k // (P * kts), P, PIECE)


def _constants():
    s = np.arange(P)
    c = np.zeros((P, NC + P), np.float32)
    c[:, C_TRI:C_TRI + P] = -(s[:, None] >= s[None, :]).astype(np.float32)
    c[:, C_ONE:C_ONE + P] = -1.0
    c[:, C_AVG:C_AVG + P] = 1.0 / P
    c[:, C_ID:C_ID + P] = np.eye(P)
    c[:, C_SBM:C_SBM + P] = np.where(s[:, None] >= s[None, :], -BIG, 0.0)
    causal = np.where(s[None, :] > s[:, None], -BIG, 0.0)
    c[:, C_CM:C_CM + P] = causal
    c[:, C_CM + 2 * P:C_CM + 3 * P] = causal
    inv = (1.0 / (np.float32(10000.0) ** (np.arange(0, P, 2, dtype=np.float32) / np.float32(P)))).astype(np.float32)
    ang = (np.arange(T, dtype=np.float32)[:, None] * inv[None, :]).T
    c[:, C_COS:C_COS + T] = np.concatenate([np.cos(ang), np.cos(ang)])
    c[:, C_SIN:C_SIN + T] = np.concatenate([np.sin(ang), -np.sin(ang)])
    c[:, NC:NC + P] = 1.0 / D
    return c


def kernel(x, attn_norm_g, ffn_norm_g, sb_w_qkv, sb_w_o, dsa_w_in, dsa_q_norm_g, dsa_k_norm_g, dsa_ik_norm_g, dsa_w_o,
           ffn_w_up, ffn_conv_w, ffn_conv_b, ffn_w_down):
    import concourse.bacc as bacc
    from concourse.bass_utils import run_bass_kernel_spmd

    a = {k: np.asarray(v) for k, v in dict(
        x=x, ag=attn_norm_g, fg=ffn_norm_g, qkv=sb_w_qkv, wo0=sb_w_o, win=dsa_w_in, qg=dsa_q_norm_g, kg=dsa_k_norm_g,
        ig=dsa_ik_norm_g, wo1=dsa_w_o, up=ffn_w_up, cw=ffn_conv_w, cb=ffn_conv_b, dn=ffn_w_down).items()}

    flat = lambda *p: [q.reshape(-1, P, PIECE) for q in p]
    qkv = [_pieces(a["qkv"][0][:, n * D:(n + 1) * D], 4, 256) for n in range(3)]
    win = a["win"][0]
    kv = KVH * P
    q, k, v, qi, kk, wi = np.split(win, np.cumsum([D, kv, kv, D, P]), axis=1)

    def mlp(layer):
        up = a["up"][layer]
        both = np.concatenate([_pieces(up[:, :FF], 2, 512), _pieces(up[:, FF:], 2, 512)], axis=1)
        return flat(both, _pieces(a["dn"][layer], 2, 512))

    qip = _pieces(qi, 4, 256)
    w_all = np.concatenate(
        flat(np.concatenate(qkv, axis=1), _pieces(a["wo0"][0], 2, 512)) + mlp(0)
        + flat(qip[:1], _pieces(kk, 8, P), _pieces(np.pad(wi, ((0, 0), (0, P - NH))), 8, P), qip[1:],
               _pieces(v, 2, 512), _pieces(k, 4, 256), _pieces(q, 4, 256),
               _pieces(a["wo1"][0], 2, 512)) + mlp(1))
    assert w_all.shape == (NPIECES, P, PIECE)

    gains = [g.reshape(KT, P).T for g in (a["ag"][0], a["fg"][0], a["ag"][1], a["fg"][1])]
    taps = np.concatenate([a["cw"], a["cb"][:, None]], axis=1)
    taps = taps.reshape(2, 4, 2, UPG, 4, P).transpose(5, 0, 3, 2, 4, 1).reshape(P, -1)
    dsa = [a[n][0] for n in ("qg", "kg", "ig")]
    vecs = np.concatenate(gains + [taps, np.stack(dsa, axis=1), np.full((P, 1), EPS, np.float32)], axis=1)
    ins = {
        "x_in": a["x"][0].T.reshape(KT, P, T).transpose(1, 0, 2),
        "w_all": w_all,
        "vecs_in": vecs,
        "consts_in": _constants(),
    }
    ins = {n: np.ascontiguousarray(v) for n, v in ins.items()}
    nc = bacc.Bacc("TRN2", target_bir_lowering=False, num_devices=1)
    aps = {n: nc.dram_tensor(n, v.shape, F32, kind="ExternalInput").ap() for n, v in ins.items()}
    out = nc.dram_tensor("out_t", (P, KT, T), F32, kind="ExternalOutput").ap()
    build(nc, **aps, out=out)
    r = run_bass_kernel_spmd(nc, [ins], core_ids=[0])
    o = r.results[0]["out_t"]
    return np.ascontiguousarray(o.transpose(2, 1, 0).reshape(1, T, D))
```
